# Optimizing a Trainium2 kernel written in Bass

```python
import jax, jax.numpy as jnp
from jax import lax
import numpy as np

D_MODEL = 1024
BATCH = 1
SEQ = 1024
DEPTH = 1

CHUNK = 128
A_GROUPS = 4
A_WIDTH = 512
A_GROUP_DIM = A_WIDTH // A_GROUPS
N_HEADS = 8
N_KV_HEADS = 2
HEAD_DIM = 64
Q_DIM = N_HEADS * HEAD_DIM
KV_DIM = N_KV_HEADS * HEAD_DIM
WINDOW = 128
BLOCK = 128
N_BUCKETS = 32
MAX_DISTANCE = 128
D_FF = 2816
CONV_WIDTH = 3
EPS = 1e-6
NEG_INF = -1e30
IN_SIZES = (A_WIDTH, A_WIDTH, Q_DIM, KV_DIM, KV_DIM, D_MODEL, D_MODEL)
IN_DIM = sum(IN_SIZES)

kernel_name = "hybrid_gated_gmlp_swa_convffn"

def rmsnorm(x, g):
    xf = x.astype(jnp.float32)
    r = lax.rsqrt(jnp.mean(xf * xf, axis=-1, keepdims=True) + EPS)
    return (xf * r * g.astype(jnp.float32)).astype(x.dtype)

def band_buckets():
    i = np.arange(BLOCK)[:, None]
    j = np.arange(2 * BLOCK)[None, :]
    dist = i + BLOCK - j
    valid = (dist >= 0) & (dist < WINDOW)
    d = np.clip(dist, 0, None)
    max_exact = N_BUCKETS // 2
    large = max_exact + (np.log(np.maximum(d, 1) / max_exact) / np.log(MAX_DISTANCE / max_exact)
                         * (N_BUCKETS - max_exact)).astype(np.int32)
    large = np.minimum(large, N_BUCKETS - 1)
    buckets = np.where(d < max_exact, d, large).astype(np.int32)
    return buckets, valid

def spatial_gating(u, v, g_sgu, w_s, b_s):
    B, S = v.shape[0], v.shape[1]
    nc = S // CHUNK
    v = rmsnorm(v, g_sgu).reshape(B, nc, CHUNK, A_GROUPS, A_GROUP_DIM)
    causal = jnp.tril(jnp.ones((CHUNK, CHUNK), dtype=w_s.dtype))
    w_masked = w_s * causal[None]
    s = jnp.einsum('gts,bcsgd->bctgd', w_masked, v) + jnp.transpose(b_s)[None, None, :, :, None]
    return u * s.reshape(B, S, A_WIDTH)

def swa_sink_attention(q, k, v, sinks, rel_bias):
    B, S = q.shape[0], q.shape[1]
    nb = S // BLOCK
    G = N_HEADS // N_KV_HEADS
    qb = q.reshape(B, nb, BLOCK, N_KV_HEADS, G, HEAD_DIM)
    kb = k.reshape(B, nb, BLOCK, N_KV_HEADS, HEAD_DIM)
    vb = v.reshape(B, nb, BLOCK, N_KV_HEADS, HEAD_DIM)
    pad = ((0, 0), (1, 0), (0, 0), (0, 0), (0, 0))
    kw = jnp.concatenate([jnp.pad(kb, pad)[:, :-1], kb], axis=2)
    vw = jnp.concatenate([jnp.pad(vb, pad)[:, :-1], vb], axis=2)
    scale = HEAD_DIM ** -0.5
    scores = jnp.einsum('bnqhgd,bnkhd->bnhgqk', qb, kw).astype(jnp.float32) * scale
    buckets, valid = band_buckets()
    bias = rel_bias[buckets].astype(jnp.float32)
    bias = jnp.transpose(bias, (2, 0, 1)).reshape(N_KV_HEADS, G, BLOCK, 2 * BLOCK)
    first_ok = (np.arange(nb)[:, None] > 0) | (np.arange(2 * BLOCK)[None, :] >= BLOCK)
    mask = valid[None, :, :] & first_ok[:, None, :]
    scores = jnp.where(mask[None, :, None, None], scores + bias[None, None], NEG_INF)
    sink = sinks.astype(jnp.float32).reshape(N_KV_HEADS, G)[None, None, :, :, None, None]
    m = jnp.maximum(jnp.max(scores, axis=-1, keepdims=True), sink)
    p = jnp.exp(scores - m)
    probs = p / (jnp.sum(p, axis=-1, keepdims=True) + jnp.exp(sink - m))
    out = jnp.einsum('bnhgqk,bnkhd->bnqhgd', probs.astype(vw.dtype), vw)
    return out.reshape(B, S, Q_DIM)

def causal_depthwise_conv(x, w, b):
    S = x.shape[1]
    xp = jnp.pad(x, ((0, 0), (CONV_WIDTH - 1, 0), (0, 0)))
    y = w[0] * xp[:, 0:S]
    for j in range(1, CONV_WIDTH):
        y = y + w[j] * xp[:, j:j + S]
    return y + b

def setup_inputs(seed: int = 0) -> dict:
    key = jax.random.key(seed)
    ks = jax.random.split(key, 20)
    f32 = jnp.float32
    nrm = lambda k, shape, s: (jax.random.normal(k, shape, f32) * s)
    L = DEPTH
    return {
        "x": nrm(ks[0], (BATCH, SEQ, D_MODEL), 1.0),
        "g_mix": 1.0 + nrm(ks[1], (L, D_MODEL), 0.05),
        "w_in": nrm(ks[2], (L, D_MODEL, IN_DIM), D_MODEL ** -0.5),
        "g_sgu": 1.0 + nrm(ks[3], (L, A_WIDTH), 0.05),
        "w_s": nrm(ks[4], (L, A_GROUPS, CHUNK, CHUNK), CHUNK ** -0.5),
        "b_s": 1.0 + nrm(ks[5], (L, A_GROUPS, CHUNK), 0.1),
        "sinks": nrm(ks[6], (L, N_HEADS), 0.5),
        "rel_bias": nrm(ks[7], (N_BUCKETS, N_HEADS), 0.5),
        "w_pa": nrm(ks[8], (L, A_WIDTH, D_MODEL), A_WIDTH ** -0.5),
        "w_pb": nrm(ks[9], (L, Q_DIM, D_MODEL), Q_DIM ** -0.5),
        "w_out": nrm(ks[10], (L, D_MODEL, D_MODEL), D_MODEL ** -0.5),
        "g_ffn": 1.0 + nrm(ks[11], (L, D_MODEL), 0.05),
        "w_up": nrm(ks[12], (L, D_MODEL, 2 * D_FF), D_MODEL ** -0.5),
        "w_conv": nrm(ks[13], (L, CONV_WIDTH, 2 * D_FF), CONV_WIDTH ** -0.5),
        "b_conv": nrm(ks[14], (L, 2 * D_FF), 0.01),
        "w_down": nrm(ks[15], (L, D_FF, D_MODEL), D_FF ** -0.5),
        "g_final": 1.0 + nrm(ks[16], (D_MODEL,), 0.05),
    }

def reference(x, g_mix, w_in, g_sgu, w_s, b_s, sinks, rel_bias, w_pa, w_pb, w_out,
              g_ffn, w_up, w_conv, b_conv, w_down, g_final):
    splits = [int(c) for c in np.cumsum(IN_SIZES)[:-1]]
    B, S = x.shape[0], x.shape[1]
    for l in range(DEPTH):
        h = rmsnorm(x, g_mix[l])
        proj = jnp.einsum('bsd,de->bse', h, w_in[l])
        pu, pv, q, k, v, gate_a, gate_b = jnp.split(proj, splits, axis=-1)
        y_a = spatial_gating(jax.nn.gelu(pu), jax.nn.gelu(pv), g_sgu[l], w_s[l], b_s[l])
        y_b = swa_sink_attention(q.reshape(B, S, N_HEADS, HEAD_DIM),
                                 k.reshape(B, S, N_KV_HEADS, HEAD_DIM),
                                 v.reshape(B, S, N_KV_HEADS, HEAD_DIM),
                                 sinks[l], rel_bias)
        merged = (jax.nn.sigmoid(gate_a) * jnp.einsum('bse,ed->bsd', y_a, w_pa[l])
                  + jax.nn.sigmoid(gate_b) * jnp.einsum('bse,ed->bsd', y_b, w_pb[l]))
        x = x + jnp.einsum('bsd,de->bse', merged, w_out[l])
        h2 = rmsnorm(x, g_ffn[l])
        up = causal_depthwise_conv(jnp.einsum('bsd,df->bsf', h2, w_up[l]), w_conv[l], b_conv[l])
        gate, val = jnp.split(up, 2, axis=-1)
        x = x + jnp.einsum('bsf,fd->bsd', jax.nn.silu(gate) * val, w_down[l])
    return rmsnorm(x, g_final)


_drawn_inputs = setup_inputs


def setup_inputs(seed=0):
    import zlib

    import numpy as np

    out = dict(_drawn_inputs(seed))
    spreads = {}
    factors = {'g_sgu': 4.707, 'sinks': 8.0, 'b_conv': 8.0}
    for name, (base, spread) in spreads.items():
        noise = np.random.default_rng([zlib.crc32(name.encode()), seed]).standard_normal(out[name].shape)
        drawn = base * np.exp(spread * noise) if base else spread * noise
        out[name] = __import__('jax').numpy.asarray(drawn.astype(out[name].dtype))
    for name, factor in factors.items():
        out[name] = (out[name] * factor).astype(out[name].dtype)
    return out
```

```python
from contextlib import ExitStack

import concourse.bass as bass
from concourse import mybir

F32 = mybir.dt.float32
F32R = mybir.dt.float32r
ACT = mybir.ActivationFunctionType
ALU = mybir.AluOpType
AX_X = mybir.AxisListType.X

P = 128
SEQ = 1024
D = 1024
AW = 512
NH = 8
NKV = 2
G = NH // NKV
HD = 64
WINDOW = 128
NBUCKET = 32
DFF = 2816
EPS = 1e-6
NEG = -1e30
NB = SEQ // P
KD = D // P
KA = AW // P
HALF = 512
NF = DFF // P
NPAIR = NF // 2
SCALE = HD ** -0.5
RC = 3 * P - 1

M_IN = 0
N_IN = 14
M_A = M_IN + N_IN
M_B = M_A + 2 * KD
M_O = M_B + 2 * KD
M_F = M_O + NB
F_O = M_O // 2
R_O = M_O
X_O = 2
R_F = R_O + KD
R_S = R_F + 2


def hybrid_block(nc, x, g_mix, w_in, g_sgu, w_s, b_s, sinks, rel_bias, bucket_rows, w_pa, w_pb, w_out,
                 g_ffn, w_up, conv, w_down, g_final, out):
    ctx = ExitStack()
    with ctx:
        def sem(name):
            return ctx.enter_context(nc.semaphore(name))

        def pair(name):
            return [sem(f"{name}0"), sem(f"{name}1")]

        BASE = 16512
        KB = 1024

        def at(name, offset, shape, dt=F32):
            return nc.alloc_sbuf_tensor_at(name, shape, dt, offset=BASE + offset)

        h_hi = at("h_hi", 0, [P, KD, SEQ], F32R)
        h_lo = at("h_lo", 32 * KB, [P, KD, SEQ], F32R)
        wo_hi = at("wo_hi", 0, [P, KD, D], F32R)
        wo_lo = at("wo_lo", 32 * KB, [P, KD, D], F32R)
        f_hi = at("f_hi", 0, [P, 2, SEQ], F32R)
        f_lo = at("f_lo", 8 * KB, [P, 2, SEQ], F32R)
        wd_hi = at("wd_hi", 16 * KB, [P, 2, D], F32R)
        wd_lo = at("wd_lo", 24 * KB, [P, 2, D], F32R)
        gfin = at("gfin", 32 * KB, [P, D])
        outbuf = at("outbuf", 36 * KB, [P, 2, D])
        fl_hi = at("fl_hi", 44 * KB, [P, 2, SEQ], F32R)
        fl_lo = at("fl_lo", 52 * KB, [P, 2, SEQ], F32R)
        y_hi = at("y_hi", 64 * KB, [P, KA, SEQ], F32R)
        y_lo = at("y_lo", 80 * KB, [P, KA, SEQ], F32R)
        resid = at("resid", 64 * KB, [P, NB, D])
        gl = at("gl", 80 * KB, [P, 2 * KA, SEQ])
        u_t = gl[:, KA:2 * KA, :]
        vn = at("vn", 112 * KB, [P, NB, AW])
        half_m = at("half_m", 96 * KB, [P, KD, SEQ])
        a_hi = at("a_hi", 96 * KB, [P, KD, SEQ], F32R)
        a_lo = at("a_lo", 128 * KB, [P, KD, SEQ], F32R)
        wdl_hi = at("wdl_hi", 96 * KB, [P, 2, D], F32R)
        wdl_lo = at("wdl_lo", 104 * KB, [P, 2, D], F32R)
        xin = at("xin", 128 * KB, [P, 4, D])
        qkv = at("qkv", 128 * KB, [P, 6, SEQ])
        v_t, k_t, q_t = qkv[:, 0, :], qkv[:, 1, :], qkv[:, 2:6, :]
        v_nat = at("v_nat", 152 * KB, [P, NB, P])
        q_st = at("q_st", 156 * KB, [P, G, P])
        k_st = at("k_st", 158 * KB, [P, 2, P])
        v_st = at("v_st", 159 * KB, [P, 2, P])
        raw = at("raw", 160 * KB, [P, 2, D])
        w_hi = at("w_hi", 168 * KB, [P, 2, KD, P], F32R)
        w_lo = at("w_lo", 176 * KB, [P, 2, KD, P], F32R)
        band = at("band", 184 * KB, [P, NH, 2 * P])
        wo_raw = at("wo_raw", 184 * KB, [P, X_O, D])
        xn2 = at("xn2", 184 * KB, [P, 2, D])
        conv_w = at("conv_w", 184 * KB, [P, 2 * NF, 4])
        g_bc = at("g_bc", 192 * KB, [P, D])
        sc = at("sc", 192 * KB, [P, G, 2 * P])
        mrg = at("mrg", 192 * KB, [P, SEQ])
        sgu_t = at("sgu_t", 192 * KB, [P, 2, AW])
        gs_bc = at("gs_bc", 196 * KB, [P, AW])
        bs_bc = at("bs_bc", 198 * KB, [P, AW])
        p_t = at("p_t", 196 * KB, [P, 2, AW])
        eb = at("eb", 200 * KB, [P, SEQ])
        c_g = [at("c_g0", 192 * KB, [P, SEQ]), at("c_g1", 196 * KB, [P, SEQ])]
        c_v = [at("c_v0", 200 * KB, [P, SEQ]), at("c_v1", 188 * KB, [P, SEQ])]
        SM = 204 * KB
        wsT = at("wsT", SM, [P, KA, P])
        ident = at("ident", SM + 2048, [P, P])
        ss = at("ss", SM + 2560, [P, NB])
        ms = at("ms", SM + 2592, [P, NB])
        rs = at("rs", SM + 2624, [P, NB])
        mhalf = at("mhalf", SM + 2656, [P, NB])
        sink = at("sink", SM + 2688, [P, NH])
        nsink = at("nsink", SM + 2720, [P, NH])
        mx = at("mx", SM + 2752, [P, G])
        nm = at("nm", SM + 2784, [P, G])
        sn = at("sn", SM + 2816, [P, G])
        es = at("es", SM + 2848, [P, G])
        lsum = at("lsum", SM + 2880, [P, G])
        den = at("den", SM + 2912, [P, G])
        rden = at("rden", SM + 2944, [P, G])
        rb = at("rb", 64 * KB, [P, NH])
        brow = at("brow", 65 * KB, [P, RC + 1])
        rrow = at("rrow", 67 * KB, [P, RC + 1])

        ps = ctx.enter_context(nc.psum_tensor("ps", [P, 2, 2, HALF], F32))
        aux = ctx.enter_context(nc.psum_tensor("aux", [P, 4, HALF], F32))

        s_raw = pair("raw_loaded")
        s_wx = sem("w_out_extra_loaded")
        s_hi = sem("weight_hi_made")
        s_lo = sem("weight_lo_made")
        s_mm = sem("chunk_multiplied")
        s_free = pair("pair_evacuated")
        s_x = [sem(f"x_loaded{i}") for i in range(4)]
        s_small = sem("smalls_loaded")
        s_gm = sem("g_mix_loaded")
        s_gs = sem("sgu_vectors_loaded")
        s_gf = sem("g_ffn_loaded")
        s_gfin = sem("g_final_loaded")
        s_conv = sem("conv_loaded")
        s_const = sem("constants_made")
        s_rrow = sem("bias_rows_ready")
        s_band = sem("band_loaded")
        s_bout = sem("bias_rows_stored")
        s_bm = sem("bias_rows_multiplied")
        s_rb = sem("bias_table_loaded")
        s_sq = sem("squares_summed")
        s_ms = sem("mean_square_ready")
        s_rs = sem("rsqrt_ready")
        s_xn = sem("block_normed")
        s_tr = sem("block_transposed")
        s_thi = sem("block_hi_made")
        s_tlo = sem("block_lo_made")
        s_vt = sem("gmlp_v_transposed")
        s_vn = sem("gmlp_v_copied")
        s_vq = sem("gmlp_v_squared")
        s_vh = sem("gmlp_v_normed")
        s_at = sem("attn_v_transposed")
        s_av = sem("attn_v_copied")
        s_sg = sem("sgu_multiplied")
        s_sb = sem("sgu_biased")
        s_yf = sem("y_a_made")
        s_yhi = sem("y_hi_made")
        s_ylo = sem("y_lo_made")
        s_st = sem("qk_staged")
        s_vst = sem("v_staged")
        s_s = sem("scores_multiplied")
        s_sc = sem("scores_biased")
        s_mx = sem("row_max_ready")
        s_nm = sem("shift_ready")
        s_sn = sem("sink_shifted")
        s_e = sem("exps_ready")
        s_den = sem("denominator_ready")
        s_p = sem("probs_ready")
        s_t = sem("probs_transposed")
        s_pt = sem("probs_copied")
        s_v = sem("values_multiplied")
        s_yb = sem("y_b_made")
        s_mg = sem("merged_ready")
        s_mhi = sem("merged_hi_made")
        s_mlo = sem("merged_lo_made")
        s_dhi = sem("block_hi_staged")
        s_dlo = sem("block_lo_staged")
        s_res = sem("residual_added")
        s_rx = pair("resid_loaded")
        s_c0 = sem("conv_tap2_done")
        s_c1 = sem("conv_tap1_done")
        s_si = sem("silu_done")
        s_f = sem("hidden_ready")
        s_fhi = sem("hidden_hi_made")
        s_flo = sem("hidden_lo_made")
        s_d = sem("down_multiplied")
        s_da = [sem(f"down_bank{b}_accumulated") for b in range(4)]
        s_ob = sem("output_normed")
        s_out = pair("output_stored")

        PITCH = NH * (RC + 1)
        scratch = nc.dram_tensor("band_rows", (P, NH, RC + 1), F32, kind="Internal").ap()
        band_src = bass.AP(scratch.tensor, P - 1, [[PITCH - 1, P], [RC + 1, NH], [1, 2 * P]])

        def bcast(v, n):
            return bass.AP(v.tensor, v.offset, [[0, P], [1, n]])

        def ge(eng, s, n):
            if not (isinstance(n, int) and n <= 0):
                eng.wait_ge(s, n)

        ctx.enter_context(nc.allow_non_contiguous_dma("band and broadcast loads"))
        block = ctx.enter_context(nc.Block())

        @block.sync
        def _(sp):
            def load(r, slot, src, cols=D):
                ge(sp, s_lo, r - 1)
                sp.dma_start(raw[:, slot, 0:cols], src).then_inc(s_raw[slot], 16)

            sp.dma_start(xin[:, 0, :], x[0]).then_inc(s_x[0], 16)
            sp.dma_start(g_bc[:, :], bcast(g_mix, D)).then_inc(s_gm, 16)
            for n in range(1, 4):
                sp.dma_start(xin[:, n, :], x[n]).then_inc(s_x[n], 16)
            load(0, 0, w_in[0])
            load(1, 1, w_in[1])
            sp.dma_start(rb[0:NBUCKET, :], rel_bias).then_inc(s_rb, 16)
            sp.dma_start(brow[0:NBUCKET + 1, :], bucket_rows).then_inc(s_rb, 16)
            for n in range(4, NB):
                sp.wait_ge(s_xn, n - 3)
                sp.dma_start(xin[:, n - 4, :], x[n]).then_inc(s_x[n - 4], 16)
            sp.dma_start(wsT[:, :, :], w_s).then_inc(s_small, 16)
            sp.dma_start(sink[:, :], bcast(sinks, NH)).then_inc(s_small, 16)
            sp.dma_start(gs_bc[:, :], bcast(g_sgu, AW)).then_inc(s_gs, 16)
            sp.dma_start(bs_bc[:, :], bcast(b_s, AW)).then_inc(s_gs, 16)
            sp.wait_ge(s_rrow, 1)
            sp.dma_start(scratch.rearrange("i h c -> h i c"),
                         rrow[0:NH, :].rearrange("h (o c) -> h o c", o=1).to_broadcast([NH, P, RC + 1])
                         ).then_inc(s_bout, 16)
            sp.wait_ge(s_bout, 16)
            sp.wait_ge(s_tr, NB)
            sp.dma_start(band[:, :, :], band_src).then_inc(s_band, 16)
            with sp.Fori(1, N_IN // 2) as t:
                for slot in range(2):
                    load(2 * t + slot, slot, w_in[2 * t + slot])
            with sp.Fori(0, KD) as d:
                load(M_A + 2 * d, 0, w_in[N_IN + d])
                load(M_A + 2 * d + 1, 1, w_pa[d], KA * P)
            with sp.Fori(0, KD) as d:
                load(M_B + 2 * d, 0, w_in[N_IN + KD + d])
                load(M_B + 2 * d + 1, 1, w_pb[d], KA * P)
            load(R_O, 0, w_out[0])
            load(R_O + 1, 1, w_out[1])
            sp.wait_ge(s_sc, 2 * NB)
            for k in range(2, 2 + X_O):
                sp.dma_start(wo_raw[:, k - 2, :], w_out[k]).then_inc(s_wx, 16)
            for k in range(2 + X_O, KD):
                sp.wait_ge(s_lo, R_O + (k - 1 - X_O if k < 4 + X_O else k - 1))
                sp.dma_start(raw[:, k % 2, :], w_out[k]).then_inc(s_raw[k % 2], 16)
            sp.wait_ge(s_mm, M_O)
            for n in range(2):
                sp.dma_start(resid[:, n, :], x[n]).then_inc(s_rx[n], 16)
            sp.wait_ge(s_mlo, KD)
            sp.dma_start(g_bc[:, :], bcast(g_ffn, D)).then_inc(s_gf, 16)
            with sp.Fori(1, NB // 2) as t:
                for slot in range(2):
                    sp.wait_ge(s_res, 2 * t + slot - 1)
                    sp.dma_start(resid[:, 2 * t + slot, :], x[2 * t + slot]).then_inc(s_rx[slot], 16)
            load(R_F, 0, w_up[0])
            load(R_F + 1, 1, w_up[NF])
            sp.wait_ge(s_tr, 2 * NB)
            sp.dma_start(conv_w[:, :, :], conv).then_inc(s_conv, 16)
            sp.wait_ge(s_mm, M_F)
            sp.dma_start(gfin[:, :], bcast(g_final, D)).then_inc(s_gfin, 16)

            def ffn_tiles(i, last):
                r = R_S + 6 * i
                load(r, 0, w_up[2 * i + 1])
                load(r + 1, 1, w_up[2 * i + (NF + 1)])
                load(r + 2, 0, w_down[2 * i])
                if last:
                    load(r + 3, 1, w_down[2 * i + 1])
                    return
                load(r + 3, 1, w_up[2 * i + 2])
                load(r + 4, 0, w_down[2 * i + 1])
                load(r + 5, 1, w_up[2 * i + (NF + 2)])

            with sp.Fori(0, NPAIR - 1) as i:
                ffn_tiles(i, False)
            ffn_tiles(NPAIR - 1, True)
            for n in range(NB):
                sp.wait_ge(s_ob, n + 1)
                sp.dma_start(out[n], outbuf[:, n % 2, :]).then_inc(s_out[n % 2], 16)
            for s in s_out:
                sp.wait_ge(s, 16 * (NB // 2))

        @block.gpsimd
        def _(pool):
            pool.memset(ident[:, :], 0.0).then_inc(s_const, 1)
            pool.memset(mhalf[:, :], -0.5).then_inc(s_const, 1)
            pool.wait_ge(s_const, 2)
            pool.memset(rb[NBUCKET:NBUCKET + 1, :], 1.0).then_inc(s_const, 1)
            pool.wait_ge(s_const, 3)
            pool.affine_select(out=ident[:, :], in_=ident[:, :], compare_op=ALU.not_equal, fill=1.0, base=0,
                               pattern=[[-1, P]], channel_multiplier=1).then_inc(s_const, 1)

            def rsqrt(count, lo, hi):
                pool.wait_ge(s_ms, count)
                pool.tensor_tensor(rs[:, lo:hi], ms[:, lo:hi], mhalf[:, lo:hi], ALU.pow).then_inc(s_rs, 1)

            with pool.Fori(0, NB // 4) as t:
                for j in range(4):
                    rsqrt(4 * t + j + 1, j, j + 1)
            pool.wait_ge(s_small, 32)
            pool.affine_select(out=wsT[:, :, :], in_=wsT[:, :, :], compare_op=ALU.is_ge, fill=0.0, base=0,
                               pattern=[[0, KA], [1, P]], channel_multiplier=-1).then_inc(s_const, 1)
            pool.memset(v_st[:, 0, :], 0.0).then_inc(s_const, 1)
            rsqrt(NB + 1, 0, NB)
            with pool.Fori(0, NB // 2) as t:
                for j in range(2):
                    rsqrt(2 * t + (NB + 2 + j), j, j + 1)
            with pool.Fori(0, NB // 2) as t:
                for j in range(2):
                    rsqrt(2 * t + (2 * NB + 2 + j), j, j + 1)

        @block.scalar
        def _(act):
            def split_hi(dst, raw_slot, cols, landed):
                act.wait_ge(s_raw[raw_slot], 16 * landed)
                act.activation(dst, raw[:, raw_slot, 0:cols], ACT.Copy).then_inc(s_hi, 1)

            def tile_hi(t, slot, k=KD, landed=None):
                ge(act, s_mm, 2 * t + (slot - 1))
                split_hi(w_hi[:, slot, 0:k, :].rearrange("p k n -> p (k n)"), slot, k * P,
                         t + 1 if landed is None else landed)

            def bank_pair(j):
                return ps[:, j, :, :].rearrange("p b n -> p (b n)")

            def in_square(n):
                j = n % 4
                act.wait_ge(s_x[j], 16 * (n // 4 + 1))
                ge(act, s_ms, n - 3)
                ge(act, s_sq, n)
                act.activation(eb[:, :], xin[:, j, :], ACT.Square, accum_out=ss[:, j:j + 1]).then_inc(s_sq, 1)

            def in_hi(n):
                act.wait_ge(s_tr, n + 1)
                j = 2 * (n % 2)
                act.activation(h_hi[:, :, n * P:(n + 1) * P],
                               aux[:, j:j + 2, :].rearrange("p b (k n) -> p (b k) n", n=P),
                               ACT.Copy).then_inc(s_thi, 1)

            in_square(0)
            in_square(1)
            for n in range(NB):
                if n + 2 < NB:
                    in_square(n + 2)
                if n in (2, 3):
                    tile_hi(0, n - 2)
                in_hi(n)

            with act.Fori(0, KA) as t:
                for j in range(2):
                    act.wait_ge(s_mm, 2 * t + (j + 1))
                    act.activation(gl[:, 2 * t + j, :], bank_pair(j), ACT.Gelu_apprx_tanh).then_inc(s_free[j], 1)
                    tile_hi(t + 1, j)
            for n in range(NB):
                act.wait_ge(s_vn, n + 1)
                act.wait_ge(s_sq, NB) if n == 0 else act.wait_ge(s_vq, n)
                act.activation(eb[:, 0:AW], vn[:, n, :], ACT.Square, accum_out=ss[:, n:n + 1]).then_inc(s_vq, 1)
            with act.Fori(KA + 1, N_IN // 2) as t:
                for j in range(2):
                    tile_hi(t, j)
            act.wait_ge(s_band, 16)
            for n in range(NB):
                act.wait_ge(s_yf, n + 1)
                act.activation(y_hi[:, :, n * P:(n + 1) * P],
                               sgu_t[:, n % 2, :].rearrange("p (c n) -> p c n", n=P), ACT.Copy).then_inc(s_yhi, 1)
            tile_hi(N_IN // 2, 0)
            tile_hi(N_IN // 2, 1, KA)

            def stage_qk(n, first=False):
                ge(act, s_s, 2 * n)
                act.activation(q_st[:, :, :], q_t[:, :, bass.ds(n * P, P)], ACT.Copy).then_inc(s_st, 1)
                if first:
                    act.activation(k_st[:, 1, :], k_t[:, 0:P], ACT.Copy).then_inc(s_st, 1)
                else:
                    act.activation(k_st[:, :, :].rearrange("p b n -> p (b n)"),
                                   k_t[:, bass.ds(n * P - P, 2 * P)], ACT.Copy).then_inc(s_st, 1)

            def stage_v(n, first=False):
                ge(act, s_v, 2 * n)
                if first:
                    act.wait_ge(s_av, 1)
                    act.activation(v_st[:, 1, :], v_nat[:, 0, :], ACT.Copy).then_inc(s_vst, 1)
                else:
                    act.activation(v_st[:, :, :].rearrange("p b n -> p (b n)"),
                                   v_nat[:, bass.ds(n - 1, 2), :].rearrange("p b n -> p (b n)"),
                                   ACT.Copy).then_inc(s_vst, 1)

            def exps(j, first=False):
                act.wait_ge(s_sn, j + 1)
                cols = slice(P, 2 * P) if first else slice(0, 2 * P)
                for h in range(G):
                    act.activation(sc[:, h, cols], sc[:, h, cols], ACT.Exp, bias=nm[:, h:h + 1],
                                   accum_out=lsum[:, h:h + 1]).then_inc(s_e, 1)
                act.activation(es[:, :], sn[:, :], ACT.Exp).then_inc(s_e, 1)

            def probs_copy(j):
                act.wait_ge(s_t, j + 1)
                act.activation(p_t[:, :, :].rearrange("p b n -> p (b n)"),
                               aux[:, 2:4, :].rearrange("p b n -> p (b n)"), ACT.Copy).then_inc(s_pt, 1)

            def gate_tanh(c):
                act.wait_ge(s_free[1], c + N_IN // 2)
                act.wait_ge(s_mm, 2 * c + (M_A + 1))
                act.activation(eb[:, :], bank_pair(0), ACT.Tanh, scale=0.5).then_inc(s_free[0], 1)

            act.wait_ge(s_free[0], N_IN // 2)
            act.wait_ge(s_free[1], N_IN // 2)
            stage_qk(0, True)

            def a_step(n, first, last):
                if not first:
                    probs_copy(2 * n - 1)
                exps(2 * n, first)
                stage_v(n, first)
                probs_copy(2 * n)
                exps(2 * n + 1, first)
                if not last:
                    stage_qk(n + 1)
                gate_tanh(n)
                tile_hi(n + (M_A // 2 + 1), 0)
                tile_hi(n + (M_A // 2 + 1), 1, KA)

            a_step(0, True, False)
            with act.Fori(1, KD - 1) as n:
                a_step(n, False, False)
            a_step(KD - 1, False, True)

            probs_copy(2 * NB - 1)
            act.wait_ge(s_yb, 2 * NB)
            act.wait_ge(s_mm, M_B)
            for c in range(KA):
                act.activation(y_hi[:, c, :], q_t[:, c, :], ACT.Copy).then_inc(s_yhi, 1)

            def merged_hi(d):
                act.wait_ge(s_mg, d + 1)
                act.activation(a_hi[:, d, :], mrg[:, :], ACT.Copy, scale=0.5).then_inc(s_mhi, 1)

            def b_step(d):
                gate_tanh(d + KD)
                tile_hi(d + (M_B // 2 + 1), 0)
                tile_hi(d + (M_B // 2 + 1), 1, KA)
                merged_hi(d)

            with act.Fori(0, KD - 1) as d:
                b_step(d)
            gate_tanh(2 * KD - 1)

            def w_out_hi(k):
                if 2 <= k < 2 + X_O:
                    act.wait_ge(s_wx, 16 * X_O)
                    act.activation(wo_hi[:, k, :], wo_raw[:, k - 2, :], ACT.Copy).then_inc(s_hi, 1)
                else:
                    split_hi(wo_hi[:, k, :], k % 2, D, (R_O + k - (X_O if k >= 2 else 0)) // 2 + 1)

            def block_hi(n, slot):
                ge(act, s_mm, n + (M_O - 1))
                act.activation(w_hi[:, slot, :, :], a_hi[:, :, bass.ds(n * P, P)].bitcast(F32),
                               ACT.Copy).then_inc(s_dhi, 1)

            def res_square(n, slot):
                act.wait_ge(s_res, n + 1)
                act.wait_ge(s_sq, n + NB)
                act.activation(eb[:, :], resid[:, n, :], ACT.Square, accum_out=ss[:, slot:slot + 1]).then_inc(s_sq, 1)

            def res_hi(n):
                act.wait_ge(s_tr, n + (NB + 1))
                act.activation(a_hi[:, :, bass.ds(n * P, P)],
                               aux[:, 0:2, :].rearrange("p b (k n) -> p (b k) n", n=P),
                               ACT.Copy).then_inc(s_thi, 1)

            act.wait_ge(s_mm, M_O - 1)
            for k in range(KD // 2):
                w_out_hi(k)
            merged_hi(KD - 1)
            for k in range(KD // 2, KD):
                w_out_hi(k)

            def o_step(t, first, last):
                for j in range(2):
                    n = 2 * t + j
                    res_square(n, j)
                    if not (first and j == 0):
                        res_hi(n - 1)
                    if last:
                        tile_hi(R_F // 2, j, landed=(R_F - X_O) // 2 + 1)
                    else:
                        block_hi(n + 2, j)

            o_step(0, True, False)
            with act.Fori(1, NB // 2 - 1) as t:
                o_step(t, False, False)
            o_step(NB // 2 - 1, False, True)
            res_hi(NB - 1)

            def conv_tap2(i, c):
                p = c // 2
                chunk = 2 * i + p if c % 2 == 0 else 2 * i + (NF + p)
                act.wait_ge(s_mm, 4 * i + (M_F + c + 1))
                ge(act, s_flo, 2 * i + (p - 1))
                act.activation((c_v if c % 2 else c_g)[p][:, :], bank_pair(c % 2), ACT.Identity,
                               bias=conv_w[:, chunk, 3:4], scale=conv_w[:, chunk, 2:3]).then_inc(s_c0, 1)

            def silu(i, p):
                act.wait_ge(s_free[0], 2 * i + (F_O + p + 1))
                act.activation(c_g[p][:, :], c_g[p][:, :], ACT.Silu).then_inc(s_si, 1)

            def hidden_hi(i, p, last=False):
                act.wait_ge(s_f, 2 * i + (p + 1))
                act.activation((fl_hi if last else f_hi)[:, p, :], c_g[p][:, :], ACT.Copy).then_inc(s_fhi, 1)

            def ffn_up_hi(i, j, slot):
                split_hi(w_hi[:, slot, :, :].rearrange("p k n -> p (k n)"), j % 2, D, 3 * i + (R_S + j - X_O) // 2 + 1)

            def ffn_down_hi(i, j, p, last=False):
                if last:
                    act.wait_ge(s_mm, M_F + 4 * NPAIR)
                else:
                    ge(act, s_d, 2 * NB * i)
                split_hi((wdl_hi if last else wd_hi)[:, p, :], j % 2, D, 3 * i + (R_S + j - X_O) // 2 + 1)

            def ffn_step(i, last=False):
                conv_tap2(i, 0)
                ffn_up_hi(i, 0, 0)
                silu(i, 0)
                conv_tap2(i, 1)
                ffn_up_hi(i, 1, 1)
                if not last:
                    ffn_down_hi(i, 2, 0)
                hidden_hi(i, 0, last)
                conv_tap2(i, 2)
                if not last:
                    ffn_up_hi(i, 3, 0)
                    ffn_down_hi(i, 4, 1)
                silu(i, 1)
                conv_tap2(i, 3)
                if not last:
                    ffn_up_hi(i, 5, 1)
                    hidden_hi(i, 1)
                else:
                    ffn_down_hi(i, 2, 0, True)
                    hidden_hi(i, 1, True)
                    ffn_down_hi(i, 3, 1, True)

            act.wait_ge(s_conv, 16)
            ffn_step(0)
            with act.Fori(1, NPAIR - 1) as i:
                ffn_step(i)
            ffn_step(NPAIR - 1, last=True)
            for n in range(NB):
                for q in (2 * n, 2 * n + 1):
                    act.wait_ge(s_da[q % 4], 4 * (NPAIR - 1) + q // 4 + 2)
                act.wait_ge(s_ms, 2 * NB + n)
                act.wait_ge(s_sq, 2 * NB + n)
                act.activation(c_v[0][:, :], resid[:, n, :], ACT.Square,
                               accum_out=ss[:, n % 2:n % 2 + 1]).then_inc(s_sq, 1)

        @block.vector
        def _(dve):
            def split_lo(dst, hi, src, made):
                dve.wait_ge(s_hi, made)
                dve.tensor_tensor(dst, src, hi.bitcast(F32), ALU.subtract).then_inc(s_lo, 1)

            def tile_lo(t, slot, k=KD):
                split_lo(w_lo[:, slot, 0:k, :].rearrange("p k n -> p (k n)"),
                         w_hi[:, slot, 0:k, :].rearrange("p k n -> p (k n)"),
                         raw[:, slot, 0:k * P], 2 * t + (slot + 1))

            def bank_pair(j):
                return ps[:, j, :, :].rearrange("p b n -> p (b n)")

            def mean_square(col, cols, width, s, count):
                dve.wait_ge(s, count)
                dve.tensor_scalar(ms[:, col:col + cols], ss[:, col:col + cols], 1.0 / width, EPS,
                                  ALU.mult, ALU.add).then_inc(s_ms, 1)

            dve.wait_ge(s_bm, 1)
            dve.tensor_copy(rrow[0:NH, 0:RC], aux[0:NH, 3, 0:RC])
            dve.memset(rrow[0:NH, RC:RC + 1], 0.0).then_inc(s_rrow, 1)

            def in_norm(n):
                dve.wait_ge(s_rs, n + 1)
                ge(dve, s_tr, n - 1)
                dve.scalar_tensor_tensor(out=xn2[:, n % 2, :], in0=xin[:, n % 4, :], scalar=rs[:, n % 4:n % 4 + 1],
                                         in1=g_bc[:, :], op0=ALU.mult, op1=ALU.mult).then_inc(s_xn, 1)

            def in_lo(n):
                dve.wait_ge(s_thi, n + 1)
                j = 2 * (n % 2)
                dve.tensor_tensor(h_lo[:, :, n * P:(n + 1) * P],
                                  aux[:, j:j + 2, :].rearrange("p b (k n) -> p (b k) n", n=P),
                                  h_hi[:, :, n * P:(n + 1) * P].bitcast(F32), ALU.subtract).then_inc(s_tlo, 1)

            mean_square(0, 1, D, s_sq, 1)
            dve.wait_ge(s_gm, 16)
            for n in range(NB):
                if n + 1 < NB:
                    mean_square((n + 1) % 4, 1, D, s_sq, n + 2)
                in_norm(n)
                if n in (3, 4):
                    tile_lo(0, n - 3)
                if n >= 1:
                    in_lo(n - 1)
            in_lo(NB - 1)
            with dve.Fori(1, KA + 1) as t:
                for j in range(2):
                    tile_lo(t, j)

            for n in range(NB):
                dve.wait_ge(s_vt, n + 1)
                dve.tensor_copy(vn[:, n, :], aux[:, n % 4, :]).then_inc(s_vn, 1)
            mean_square(0, NB, AW, s_vq, NB)
            dve.wait_ge(s_rs, NB + 1)
            dve.wait_ge(s_gs, 32)
            for n in range(NB):
                dve.scalar_tensor_tensor(out=vn[:, n, :], in0=vn[:, n, :], scalar=rs[:, n:n + 1],
                                         in1=gs_bc[:, :], op0=ALU.mult, op1=ALU.mult).then_inc(s_vh, 1)

            def qkv_out(t, j):
                dve.wait_ge(s_mm, 2 * t + (j + 1))
                dve.tensor_copy(qkv[:, 2 * t + (j - 2 * KA), :], bank_pair(j)).then_inc(s_free[j], 1)

            with dve.Fori(KA, N_IN // 2 - 1) as t:
                for j in range(2):
                    qkv_out(t, j)
                    tile_lo(t + 1, j)
            dve.wait_ge(s_at, 1)
            dve.tensor_copy(v_nat[:, :, :].rearrange("p b n -> p (b n)"),
                            aux[:, 0:2, :].rearrange("p b n -> p (b n)")).then_inc(s_av, 1)

            def y_a_lo(n):
                dve.wait_ge(s_yhi, n + 1)
                dve.tensor_tensor(y_lo[:, :, n * P:(n + 1) * P],
                                  sgu_t[:, n % 2, :].rearrange("p (c n) -> p c n", n=P),
                                  y_hi[:, :, n * P:(n + 1) * P].bitcast(F32), ALU.subtract).then_inc(s_ylo, 1)

            for n in range(NB):
                dve.wait_ge(s_sg, n + 1)
                ge(dve, s_ylo, n - 1)
                dve.tensor_tensor(sgu_t[:, n % 2, :], aux[:, (n + 2) % 4, :], bs_bc[:, :], ALU.add).then_inc(s_sb, 1)
                if n >= 1:
                    y_a_lo(n - 1)
                t3 = sgu_t[:, n % 2, :].rearrange("p (c n) -> p c n", n=P)
                dve.wait_ge(s_sb, n + 1)
                dve.tensor_tensor(t3, t3, u_t[:, :, n * P:(n + 1) * P], ALU.mult).then_inc(s_yf, 1)
            y_a_lo(NB - 1)
            for j in range(2):
                qkv_out(N_IN // 2 - 1, j)
            tile_lo(N_IN // 2, 0)
            tile_lo(N_IN // 2, 1, KA)
            dve.wait_ge(s_small, 32)
            dve.tensor_scalar(nsink[:, :], sink[:, :], -1.0, None, ALU.mult).then_inc(s_const, 1)

            def softmax(n, g, first):
                j = 2 * n + g
                lo = P if first else 0
                s4 = sc[:, :, lo:2 * P]
                dve.wait_ge(s_s, j + 1)
                dve.scalar_tensor_tensor(out=s4, in0=aux[:, 0:2, :].rearrange("p b (h k) -> p (b h) k", k=2 * P)[:, :, lo:2 * P],
                                         scalar=SCALE, in1=band[:, g * G:(g + 1) * G, lo:2 * P],
                                         op0=ALU.mult, op1=ALU.add).then_inc(s_sc, 1)
                dve.wait_ge(s_sc, j + 1)
                dve.tensor_reduce(mx[:, :], s4, AX_X, ALU.max).then_inc(s_mx, 1)
                dve.wait_ge(s_mx, j + 1)
                dve.scalar_tensor_tensor(out=nm[:, :], in0=mx[:, :], scalar=-1.0, in1=nsink[:, g * G:(g + 1) * G],
                                         op0=ALU.mult, op1=ALU.min).then_inc(s_nm, 1)
                dve.wait_ge(s_nm, j + 1)
                dve.tensor_tensor(sn[:, :], sink[:, g * G:(g + 1) * G], nm[:, :], ALU.add).then_inc(s_sn, 1)

            def normalise(n, g, first):
                j = 2 * n + g
                lo = P if first else 0
                dve.wait_ge(s_e, (G + 1) * j + (G + 1))
                dve.tensor_tensor(den[:, :], lsum[:, :], es[:, :], ALU.add).then_inc(s_den, 1)
                dve.wait_ge(s_den, 2 * j + 1)
                dve.reciprocal(rden[:, :], den[:, :]).then_inc(s_den, 1)
                dve.wait_ge(s_den, 2 * j + 2)
                for h in range(G):
                    dve.tensor_scalar(sc[:, h, lo:2 * P], sc[:, h, lo:2 * P], rden[:, h:h + 1], None,
                                      ALU.mult).then_inc(s_p, 1)

            def y_b(n, g):
                dve.wait_ge(s_v, 2 * n + (g + 1))
                rows = slice(g * HD, (g + 1) * HD)
                dve.tensor_copy(q_t[rows, :, bass.ds(n * P, P)],
                                aux[rows, 2, :].rearrange("p (c n) -> p c n", n=P)).then_inc(s_yb, 1)

            def a_step(n, first):
                softmax(n, 0, first)
                if not first:
                    y_b(n - 1, 1)
                normalise(n, 0, first)
                softmax(n, 1, first)
                y_b(n, 0)
                normalise(n, 1, first)
                tile_lo(n + (M_A // 2 + 1), 0)
                dve.wait_ge(s_mm, 2 * n + (M_A + 2))
                dve.wait_ge(s_free[0], n + (N_IN // 2 + 1))
                dve.scalar_tensor_tensor(out=half_m[:, n, :], in0=eb[:, :], scalar=1.0, in1=bank_pair(1),
                                         op0=ALU.add, op1=ALU.mult).then_inc(s_free[1], 1)
                tile_lo(n + (M_A // 2 + 1), 1, KA)

            dve.wait_ge(s_band, 16)
            dve.wait_ge(s_const, 7)
            dve.memset(sc[:, :, 0:P], 0.0)
            a_step(0, True)
            with dve.Fori(1, KD) as n:
                a_step(n, False)

            y_b(NB - 1, 1)
            for c in range(KA):
                dve.wait_ge(s_yhi, NB + c + 1)
                dve.tensor_tensor(y_lo[:, c, :], q_t[:, c, :], y_hi[:, c, :].bitcast(F32),
                                  ALU.subtract).then_inc(s_ylo, 1)

            def b_merge(d):
                dve.wait_ge(s_mm, 2 * d + (M_B + 2))
                dve.wait_ge(s_free[0], d + (M_B // 2 + 1))
                ge(dve, s_mlo, d)
                dve.scalar_tensor_tensor(out=mrg[:, :], in0=eb[:, :], scalar=1.0, in1=bank_pair(1),
                                         op0=ALU.add, op1=ALU.mult).then_inc(s_free[1], 1)
                dve.wait_ge(s_free[1], d + (M_B // 2 + 1))
                dve.tensor_tensor(mrg[:, :], mrg[:, :], half_m[:, d, :], ALU.add).then_inc(s_mg, 1)

            def merged_lo(d):
                dve.wait_ge(s_mhi, d + 1)
                dve.scalar_tensor_tensor(out=a_lo[:, d, :], in0=mrg[:, :], scalar=0.5,
                                         in1=a_hi[:, d, :].bitcast(F32),
                                         op0=ALU.mult, op1=ALU.subtract).then_inc(s_mlo, 1)

            def b_step(d):
                tile_lo(d + (M_B // 2 + 1), 0)
                b_merge(d)
                tile_lo(d + (M_B // 2 + 1), 1, KA)
                merged_lo(d)

            b_step(0)
            with dve.Fori(1, KD - 1) as d:
                b_step(d)

            def w_out_lo(k):
                split_lo(wo_lo[:, k, :], wo_hi[:, k, :], wo_raw[:, k - 2, :] if 2 <= k < 2 + X_O else raw[:, k % 2, :],
                         R_O + k + 1)

            def block_lo(n, slot):
                dve.wait_ge(s_dhi, n - 1)
                dve.tensor_copy(w_lo[:, slot, :, :], a_lo[:, :, bass.ds(n * P, P)].bitcast(F32)).then_inc(s_dlo, 1)

            def residual(n, j):
                dve.wait_ge(s_mm, n + (M_O + 1))
                dve.wait_ge(s_rx[j], (n - j) * 8 + 16)
                dve.tensor_tensor(resid[:, n, :], bank_pair(j), resid[:, n, :], ALU.add).then_inc(s_res, 1)
                dve.wait_ge(s_res, n + 1)

            def res_norm(n, j):
                dve.wait_ge(s_rs, n + (NB + 2))
                dve.wait_ge(s_tr, n + (NB - 1))
                dve.scalar_tensor_tensor(out=xn2[:, j, :], in0=resid[:, n, :], scalar=rs[:, j:j + 1],
                                         in1=g_bc[:, :], op0=ALU.mult, op1=ALU.mult).then_inc(s_xn, 1)

            def res_lo(n):
                dve.wait_ge(s_thi, n + (NB + 1))
                dve.tensor_tensor(a_lo[:, :, bass.ds(n * P, P)],
                                  aux[:, 0:2, :].rearrange("p b (k n) -> p (b k) n", n=P),
                                  a_hi[:, :, bass.ds(n * P, P)].bitcast(F32), ALU.subtract).then_inc(s_tlo, 1)

            for k in range(KD // 2):
                w_out_lo(k)
            b_merge(KD - 1)
            merged_lo(KD - 1)
            for k in range(KD // 2, KD):
                w_out_lo(k)
            dve.wait_ge(s_gf, 16)

            def o_step(t, first, last):
                for j in range(2):
                    n = 2 * t + j
                    residual(n, j)
                    dve.wait_ge(s_sq, n + (NB + 1))
                    mean_square(j, 1, D, s_sq, n + (NB + 1))
                    if not (first and j == 0):
                        res_lo(n - 1)
                    if last:
                        tile_lo(R_F // 2, j)
                    else:
                        block_lo(n + 2, j)
                    res_norm(n, j)

            o_step(0, True, False)
            with dve.Fori(1, NB // 2 - 1) as t:
                o_step(t, False, False)
            o_step(NB // 2 - 1, False, True)
            res_lo(NB - 1)

            def accumulate(i, q):
                dve.wait_ge(s_d, 2 * NB * i + (q + 1))
                r = resid[:, q // 2, (q % 2) * HALF:(q % 2 + 1) * HALF]
                dve.tensor_tensor(r, aux[:, q % 4, :], r, ALU.add).then_inc(s_da[q % 4], 1)

            def conv_taps(i, c, between=None):
                p = c // 2
                chunk = 2 * i + p if c % 2 == 0 else 2 * i + (NF + p)
                buf = (c_v if c % 2 else c_g)[p]
                dve.wait_ge(s_c0, 4 * i + (c + 1))
                dve.scalar_tensor_tensor(out=buf[:, 1:SEQ], in0=bank_pair(c % 2)[:, 0:SEQ - 1],
                                         scalar=conv_w[:, chunk, 1:2], in1=buf[:, 1:SEQ],
                                         op0=ALU.mult, op1=ALU.add).then_inc(s_c1, 1)
                if between is not None:
                    accumulate(i - 1, between)
                dve.wait_ge(s_c1, 4 * i + (c + 1))
                dve.scalar_tensor_tensor(out=buf[:, 2:SEQ], in0=bank_pair(c % 2)[:, 0:SEQ - 2],
                                         scalar=conv_w[:, chunk, 0:1], in1=buf[:, 2:SEQ],
                                         op0=ALU.mult, op1=ALU.add).then_inc(s_free[c % 2], 1)

            def hidden(i, p):
                dve.wait_ge(s_free[1], 2 * i + (F_O + p + 1))
                dve.wait_ge(s_si, 2 * i + (p + 1))
                dve.tensor_tensor(c_g[p][:, :], c_g[p][:, :], c_v[p][:, :], ALU.mult).then_inc(s_f, 1)

            def hidden_lo(i, p, last=False):
                dve.wait_ge(s_fhi, 2 * i + (p + 1))
                lo, hi = (fl_lo, fl_hi) if last else (f_lo, f_hi)
                dve.tensor_tensor(lo[:, p, :], c_g[p][:, :], hi[:, p, :].bitcast(F32),
                                  ALU.subtract).then_inc(s_flo, 1)

            def ffn_up_lo(i, j, slot):
                split_lo(w_lo[:, slot, :, :].rearrange("p k n -> p (k n)"),
                         w_hi[:, slot, :, :].rearrange("p k n -> p (k n)"), raw[:, j % 2, :], 6 * i + (R_S + j + 1))

            def ffn_down_lo(i, j, p, last=False):
                lo, hi = (wdl_lo, wdl_hi) if last else (wd_lo, wd_hi)
                split_lo(lo[:, p, :], hi[:, p, :], raw[:, j % 2, :], 6 * i + (R_S + j + 1))

            def ffn_step(i, first=False, last=False):
                if first or last:
                    conv_taps(i, 0)
                    ffn_up_lo(i, 0, 0)
                else:
                    conv_taps(i, 0, 0)
                    for q in range(1, 4):
                        accumulate(i - 1, q)
                    ffn_up_lo(i, 0, 0)
                    for q in range(4, 2 * NB):
                        accumulate(i - 1, q)
                conv_taps(i, 1)
                hidden(i, 0)
                ffn_up_lo(i, 1, 1)
                if not last:
                    ffn_down_lo(i, 2, 0)
                hidden_lo(i, 0, last)
                conv_taps(i, 2)
                if not last:
                    ffn_up_lo(i, 3, 0)
                    ffn_down_lo(i, 4, 1)
                    conv_taps(i, 3)
                    hidden(i, 1)
                    ffn_up_lo(i, 5, 1)
                    hidden_lo(i, 1)
                else:
                    conv_taps(i, 3, 0)
                    accumulate(i - 1, 1)
                    hidden(i, 1)
                    accumulate(i - 1, 2)
                    accumulate(i - 1, 3)
                    ffn_down_lo(i, 2, 0, True)
                    accumulate(i - 1, 4)
                    accumulate(i - 1, 5)
                    hidden_lo(i, 1, True)
                    accumulate(i - 1, 6)
                    accumulate(i - 1, 7)
                    ffn_down_lo(i, 3, 1, True)
                    for q in range(8, 2 * NB):
                        accumulate(i - 1, q)

            for b in range(4):
                dve.sem_inc(s_da[b], 1)
            ffn_step(0, first=True)
            with dve.Fori(1, NPAIR - 1) as i:
                ffn_step(i)
            ffn_step(NPAIR - 1, last=True)

            def final_norm(n):
                mean_square(n % 2, 1, D, s_sq, 2 * NB + n + 1)
                dve.wait_ge(s_rs, 2 * NB + n + 2)
                ge(dve, s_out[n % 2], 16 * (n // 2))
                dve.scalar_tensor_tensor(out=outbuf[:, n % 2, :], in0=resid[:, n, :], scalar=rs[:, n % 2:n % 2 + 1],
                                         in1=gfin[:, :], op0=ALU.mult, op1=ALU.mult).then_inc(s_ob, 1)

            dve.wait_ge(s_gfin, 16)
            for n in range(NB):
                for q in (2 * n, 2 * n + 1):
                    accumulate(NPAIR - 1, q)
                if n >= 1:
                    final_norm(n - 1)
            final_norm(NB - 1)

        @block.tensor
        def _(pe):
            def product(dst, s_hi_ap, s_lo_ap, m_hi, m_lo, first, last):
                pe.matmul(dst, s_lo_ap, m_hi, start=first, stop=False)
                pe.matmul(dst, s_hi_ap, m_lo, start=False, stop=False)
                return pe.matmul(dst, s_hi_ap, m_hi, start=False, stop=last)

            def chunk_part(slot, acts_hi, acts_lo, kn, half, ks):
                cols = slice(half * HALF, (half + 1) * HALF)
                for k in ks:
                    mm = product(ps[:, slot, half, :], w_hi[:, slot, k, :], w_lo[:, slot, k, :],
                                 acts_hi[:, k, cols], acts_lo[:, k, cols], k == 0, k == kn - 1)
                return mm

            def chunk(slot, acts_hi, acts_lo, kn=KD):
                for half in range(2):
                    mm = chunk_part(slot, acts_hi, acts_lo, kn, half, range(kn))
                mm.then_inc(s_mm, 1)

            def ready(r, slot, freed):
                pe.wait_ge(s_lo, r + 1)
                pe.wait_ge(s_free[slot], freed)

            def transposes(src, pairs):
                for k in range(KD):
                    mm = pe.transpose(aux[:, pairs + k // 4, (k % 4) * P:(k % 4 + 1) * P],
                                      src[:, k * P:(k + 1) * P], ident[:, :])
                mm.then_inc(s_tr, 1)

            pe.wait_ge(s_const, 4)
            pe.wait_ge(s_rb, 32)
            pe.matmul(aux[0:NH, 3, 0:RC], rb[0:NBUCKET + 1, :], brow[0:NBUCKET + 1, 0:RC],
                      start=True, stop=True).then_inc(s_bm, 1)

            def in_transpose(n, j):
                pe.wait_ge(s_xn, n + 1)
                ge(pe, s_tlo, n - 1)
                transposes(xn2[:, j, :], 2 * j)

            in_transpose(0, 0)
            pe.wait_ge(s_rrow, 1)
            in_transpose(1, 1)
            with pe.Fori(1, NB // 2) as t:
                for j in range(2):
                    in_transpose(2 * t + j, j)

            def in_pair(t):
                for j in range(2):
                    pe.wait_ge(s_lo, 2 * t + (j + 1))
                    ge(pe, s_free[j], t)
                    chunk(j, h_hi, h_lo)

            pe.wait_ge(s_tlo, NB)
            in_pair(0)
            with pe.Fori(1, KA) as t:
                in_pair(t)
            for j in range(2):
                pe.wait_ge(s_free[j], 2)
            for n in range(NB):
                ge(pe, s_vn, n - 3)
                for c in range(KA):
                    mm = pe.transpose(aux[:, n % 4, c * P:(c + 1) * P], gl[:, c, n * P:(n + 1) * P], ident[:, :])
                mm.then_inc(s_vt, 1)
            with pe.Fori(KA, N_IN // 2 - 1) as t:
                in_pair(t)
            pe.wait_ge(s_vn, NB)
            pe.wait_ge(s_free[0], KA + 1)
            for n in range(NB):
                mm = pe.transpose(aux[:, n // 4, (n % 4) * P:(n % 4 + 1) * P], v_t[:, n * P:(n + 1) * P], ident[:, :])
            mm.then_inc(s_at, 1)
            pe.wait_ge(s_const, 5)
            for n in range(NB):
                pe.wait_ge(s_vh, n + 1)
                if n == 2:
                    pe.wait_ge(s_av, 1)
                ge(pe, s_sb, n - 3)
                for g in range(KA):
                    mm = pe.matmul(aux[:, (n + 2) % 4, g * P:(g + 1) * P], vn[:, n, g * P:(g + 1) * P],
                                   wsT[:, g, :], start=True, stop=True)
                mm.then_inc(s_sg, 1)
            in_pair(N_IN // 2 - 1)
            pe.wait_ge(s_sb, NB)

            def scores(n, g, first):
                j = 2 * n + g
                pe.wait_ge(s_st, 2 * n + 2)
                ge(pe, s_sc, j)
                rows = slice(g * HD, (g + 1) * HD)
                lo = 1 if first else 0
                for h in range(G):
                    mm = pe.matmul(aux[:, h // 2, (h % 2) * 2 * P + lo * P:(h % 2 + 1) * 2 * P],
                                   q_st[rows, h, :], k_st[rows, lo:2, :].rearrange("p b n -> p (b n)"),
                                   start=True, stop=True)
                mm.then_inc(s_s, 1)

            def probs_t(n, g):
                j = 2 * n + g
                pe.wait_ge(s_p, G * j + G)
                ge(pe, s_yb, j)
                for b in range(2):
                    for h in range(G):
                        mm = pe.transpose(aux[:, 2 + b, h * P:(h + 1) * P], sc[:, h, b * P:(b + 1) * P], ident[:, :])
                mm.then_inc(s_t, 1)

            def values(n, g):
                j = 2 * n + g
                pe.wait_ge(s_vst, n + 1)
                pe.wait_ge(s_pt, j + 1)
                rows = slice(g * HD, (g + 1) * HD)
                for b in range(2):
                    mm = pe.matmul(aux[rows, 2, :], v_st[:, b, rows], p_t[:, b, :], start=b == 0, stop=b == 1)
                mm.then_inc(s_v, 1)

            def a_step(n, first):
                if not first:
                    probs_t(n - 1, 1)
                scores(n, 0, first)
                ready(2 * n + M_A, 0, n + M_A // 2)
                chunk_part(0, h_hi, h_lo, KD, 0, range(0, 4))
                if not first:
                    values(n - 1, 1)
                chunk_part(0, h_hi, h_lo, KD, 0, range(4, 8))
                chunk_part(0, h_hi, h_lo, KD, 1, range(0, 4))
                probs_t(n, 0)
                scores(n, 1, first)
                chunk_part(0, h_hi, h_lo, KD, 1, range(4, 8)).then_inc(s_mm, 1)
                values(n, 0)
                ready(2 * n + (M_A + 1), 1, n + M_A // 2)
                chunk(1, y_hi, y_lo, KA)

            pe.wait_ge(s_const, 6)
            pe.wait_ge(s_ylo, NB)
            a_step(0, True)
            with pe.Fori(1, KD) as n:
                a_step(n, False)

            probs_t(NB - 1, 1)
            ready(M_B, 0, M_B // 2)
            chunk_part(0, h_hi, h_lo, KD, 0, range(0, 4))
            values(NB - 1, 1)
            chunk_part(0, h_hi, h_lo, KD, 0, range(4, 8))
            chunk_part(0, h_hi, h_lo, KD, 1, range(0, 8)).then_inc(s_mm, 1)
            pe.wait_ge(s_ylo, NB + KA)
            ready(M_B + 1, 1, M_B // 2)
            chunk(1, y_hi, y_lo, KA)
            with pe.Fori(1, KD) as d:
                ready(2 * d + M_B, 0, d + M_B // 2)
                chunk(0, h_hi, h_lo)
                ready(2 * d + (M_B + 1), 1, d + M_B // 2)
                chunk(1, y_hi, y_lo, KA)

            def out_part(j, k, hi, lo):
                for e in range(2):
                    cols = slice(e * HALF, (e + 1) * HALF)
                    mm = product(ps[:, j, e, :], hi, lo, wo_hi[:, k, cols], wo_lo[:, k, cols], k == 0, k == KD - 1)
                return mm

            def out_first(n):
                pe.wait_ge(s_free[n], F_O)
                for k in range(KD):
                    pe.wait_ge(s_lo, R_O + k + 1)
                    pe.wait_ge(s_mlo, KD if k == KD - 1 else KD - 1)
                    mm = out_part(n, k, a_hi[:, k, n * P:(n + 1) * P], a_lo[:, k, n * P:(n + 1) * P])
                mm.then_inc(s_mm, 1)

            def out_block(n, j):
                pe.wait_ge(s_dlo, n - 1)
                pe.wait_ge(s_res, n - 1)
                for k in range(KD):
                    mm = out_part(j, k, w_hi[:, j, k, :], w_lo[:, j, k, :])
                mm.then_inc(s_mm, 1)

            def res_transpose(n, j):
                pe.wait_ge(s_xn, n + (NB + 1))
                pe.wait_ge(s_tlo, n + NB)
                transposes(xn2[:, j, :], 0)

            out_first(0)
            out_first(1)
            res_transpose(0, 0)
            with pe.Fori(1, NB // 2) as t:
                out_block(2 * t, 0)
                res_transpose(2 * t - 1, 1)
                out_block(2 * t + 1, 1)
                res_transpose(2 * t, 0)

            def up(i, c, r):
                pe.wait_ge(s_lo, r + 1)
                pe.wait_ge(s_free[c % 2], 2 * i + (F_O + c // 2))
                chunk(c % 2, a_hi, a_lo)

            def down(i, made, fh, fl, wh, wl):
                pe.wait_ge(s_lo, made)
                pe.wait_ge(s_flo, 2 * i + 2)
                for q in range(2 * NB):
                    n, e = q // 2, q % 2
                    pe.wait_ge(s_da[q % 4], 4 * i + (q // 4 + 1))
                    for p in range(2):
                        mm = product(aux[:, q % 4, :], fh[:, p, n * P:(n + 1) * P], fl[:, p, n * P:(n + 1) * P],
                                     wh[:, p, e * HALF:(e + 1) * HALF], wl[:, p, e * HALF:(e + 1) * HALF],
                                     p == 0, p == 1)
                    mm.then_inc(s_d, 1)

            pe.wait_ge(s_lo, R_F + 1)
            pe.wait_ge(s_res, NB - 1)
            pe.wait_ge(s_tlo, NB + NB // 2)
            chunk_part(0, a_hi, a_lo, KD, 0, range(KD))
            res_transpose(NB - 1, 1)
            pe.wait_ge(s_tlo, 2 * NB)
            chunk_part(0, a_hi, a_lo, KD, 1, range(KD)).then_inc(s_mm, 1)
            pe.wait_ge(s_res, NB)
            up(0, 1, R_F + 1)
            up(0, 2, R_S)
            up(0, 3, R_S + 1)
            with pe.Fori(1, NPAIR - 1) as i:
                up(i, 0, 6 * i + (R_S - 3))
                down(i - 1, 6 * i + (R_S - 1), f_hi, f_lo, wd_hi, wd_lo)
                up(i, 1, 6 * i + (R_S - 1))
                up(i, 2, 6 * i + R_S)
                up(i, 3, 6 * i + (R_S + 1))
            i = NPAIR - 1
            up(i, 0, 6 * i + (R_S - 3))
            up(i, 1, 6 * i + (R_S - 1))
            up(i, 2, 6 * i + R_S)
            up(i, 3, 6 * i + (R_S + 1))
            down(i - 1, 6 * i + (R_S - 1), f_hi, f_lo, wd_hi, wd_lo)
            down(i, 6 * i + (R_S + 4), fl_hi, fl_lo, wdl_hi, wdl_lo)


def kernel(x, g_mix, w_in, g_sgu, w_s, b_s, sinks, rel_bias, w_pa, w_pb, w_out, g_ffn, w_up, w_conv, b_conv,
           w_down, g_final):
    import numpy as np
    import concourse.bacc as bacc
    from concourse import bass_utils

    def stationary(w):
        k, n = w.shape
        return w.reshape(k // P, P, n // P, P).transpose(2, 1, 0, 3).reshape(n // P, P, k)

    def head_pairs(a):
        return np.ascontiguousarray(a.reshape(NKV, G, HD, -1).transpose(1, 0, 2, 3)).reshape(NH * HD, -1)

    wi = w_in[0]
    pu, pv, q, k, v, gates = np.split(wi, [AW, 2 * AW, 3 * AW, 3 * AW + P, 3 * AW + 2 * P], axis=1)
    q = head_pairs(q.T).T
    w_in_t = stationary(np.concatenate([pv, pu, v, k, q, gates], axis=1))

    dist = 2 * P - 1 - np.arange(RC + 1)
    valid = (dist >= 0) & (dist < WINDOW)
    exact = NBUCKET // 2
    d = np.clip(dist, 0, None)
    large = exact + (np.log(np.maximum(d, 1) / exact) / np.log(WINDOW / exact) * (NBUCKET - exact)).astype(np.int32)
    bucket = np.where(d < exact, d, np.minimum(large, NBUCKET - 1))
    rows = np.zeros((NBUCKET + 1, RC + 1), np.float32)
    rows[bucket[valid], np.nonzero(valid)[0]] = 1.0
    rows[NBUCKET, ~valid] = NEG

    arrays = {
        "x": x[0].reshape(NB, P, D), "g_mix": g_mix[0], "w_in": w_in_t, "g_sgu": g_sgu[0],
        "w_s": w_s[0].transpose(2, 0, 1), "b_s": b_s[0].reshape(-1), "sinks": sinks[0], "rel_bias": rel_bias,
        "bucket_rows": rows, "w_pa": stationary(w_pa[0]), "w_pb": stationary(head_pairs(w_pb[0])),
        "w_out": w_out[0].reshape(KD, P, D), "g_ffn": g_ffn[0], "w_up": stationary(w_up[0]),
        "conv": np.concatenate([w_conv[0], b_conv], axis=0).reshape(4, 2 * NF, P).transpose(2, 1, 0),
        "w_down": w_down[0].reshape(NF, P, D), "g_final": g_final,
    }
    arrays = {f"in_{n}": np.ascontiguousarray(a) for n, a in arrays.items()}
    nc = bacc.Bacc("TRN2", target_bir_lowering=False, num_devices=1)
    aps = [nc.dram_tensor(n, a.shape, mybir.dt.from_np(a.dtype), kind="ExternalInput").ap()
           for n, a in arrays.items()]
    o = nc.dram_tensor("out_0_dram", (NB, P, D), F32, kind="ExternalOutput").ap()
    hybrid_block(nc, *aps, o)
    r = bass_utils.run_bass_kernel_spmd(nc, [arrays], core_ids=[0])
    return r.results[0]["out_0_dram"].reshape(1, SEQ, D)
```

```python
from contextlib import ExitStack

import concourse.bass as bass
from concourse import mybir

F32 = mybir.dt.float32
F32R = mybir.dt.float32r
ACT = mybir.ActivationFunctionType
ALU = mybir.AluOpType
AX_X = mybir.AxisListType.X

P = 128
SEQ = 1024
D = 1024
AW = 512
NH = 8
NKV = 2
G = NH // NKV
HD = 64
WINDOW = 128
NBUCKET = 32
DFF = 2816
EPS = 1e-6
NEG = -1e30
NB = SEQ // P
KD = D // P
KA = AW // P
HALF = 512
NF = DFF // P
NPAIR = NF // 2
SCALE = HD ** -0.5
RC = 3 * P - 1

M_IN = 0
N_IN = 14
M_A = M_IN + N_IN
M_B = M_A + 2 * KD
M_O = M_B + 2 * KD
M_F = M_O + NB
F_O = M_O // 2
R_O = M_O
X_O = 4
R_F = R_O + KD
R_S = R_F + 2


def hybrid_block(nc, x, g_mix, w_in, g_sgu, w_s, b_s, sinks, rel_bias, bucket_rows, w_pa, w_pb, w_out,
                 g_ffn, w_up, conv, w_down, g_final, out):
    ctx = ExitStack()
    with ctx:
        def sem(name):
            return ctx.enter_context(nc.semaphore(name))

        def pair(name):
            return [sem(f"{name}0"), sem(f"{name}1")]

        BASE = 16512
        KB = 1024

        def at(name, offset, shape, dt=F32):
            return nc.alloc_sbuf_tensor_at(name, shape, dt, offset=BASE + offset)

        h_hi = at("h_hi", 0, [P, KD, SEQ], F32R)
        h_lo = at("h_lo", 32 * KB, [P, KD, SEQ], F32R)
        wo_hi = at("wo_hi", 0, [P, KD, D], F32R)
        wo_lo = at("wo_lo", 32 * KB, [P, KD, D], F32R)
        f_hi = at("f_hi", 0, [P, 2, SEQ], F32R)
        f_lo = at("f_lo", 8 * KB, [P, 2, SEQ], F32R)
        wd_hi = at("wd_hi", 16 * KB, [P, 2, D], F32R)
        wd_lo = at("wd_lo", 24 * KB, [P, 2, D], F32R)
        gfin = at("gfin", 32 * KB, [P, D])
        outbuf = at("outbuf", 36 * KB, [P, 2, D])
        fl_hi = at("fl_hi", 44 * KB, [P, 2, SEQ], F32R)
        fl_lo = at("fl_lo", 52 * KB, [P, 2, SEQ], F32R)
        y_hi = at("y_hi", 64 * KB, [P, KA, SEQ], F32R)
        y_lo = at("y_lo", 80 * KB, [P, KA, SEQ], F32R)
        resid = at("resid", 64 * KB, [P, NB, D])
        gl = at("gl", 80 * KB, [P, 2 * KA, SEQ])
        u_t = gl[:, KA:2 * KA, :]
        vn = at("vn", 112 * KB, [P, NB, AW])
        half_m = at("half_m", 96 * KB, [P, KD, SEQ])
        a_hi = at("a_hi", 96 * KB, [P, KD, SEQ], F32R)
        a_lo = at("a_lo", 128 * KB, [P, KD, SEQ], F32R)
        wdl_hi = at("wdl_hi", 96 * KB, [P, 2, D], F32R)
        wdl_lo = at("wdl_lo", 104 * KB, [P, 2, D], F32R)
        xin = at("xin", 128 * KB, [P, NB, D])
        qkv = at("qkv", 128 * KB, [P, 6, SEQ])
        v_t, k_t, q_t = qkv[:, 0, :], qkv[:, 1, :], qkv[:, 2:6, :]
        v_nat = at("v_nat", 152 * KB, [P, NB, P])
        q_st = at("q_st", 156 * KB, [P, NKV, G, P], F32R)
        k_hi = at("k_hi", 124 * KB, [P, NKV, 2, P], F32R)
        k_lo = at("k_lo", 126 * KB, [P, 2, P], F32R)
        raw = at("raw", 160 * KB, [P, 2, D])
        w_hi = at("w_hi", 168 * KB, [P, 2, KD, P], F32R)
        w_lo = at("w_lo", 176 * KB, [P, 2, KD, P], F32R)
        y_part = at("y_part", 174 * KB, [P, AW])
        band = at("band", 184 * KB, [P, NH, 2 * P])
        wo_raw = [at(f"wo_raw{i}", place * KB, [P, D])[:, :] for i, place in enumerate((184, 188, 196, 156))]
        xn2 = at("xn2", 184 * KB, [P, 2, D])
        conv_w = at("conv_w", 184 * KB, [P, 2 * NF, 4])
        g_bc = at("g_bc", 192 * KB, [P, D])
        sc = at("sc", 192 * KB, [P, G, 2 * P])
        mrg = at("mrg", 192 * KB, [P, SEQ])
        sgu_t = at("sgu_t", 192 * KB, [P, 2, AW])
        gs_bc = at("gs_bc", 196 * KB, [P, AW])
        bs_bc = at("bs_bc", 198 * KB, [P, AW])
        p_hi = at("p_hi", 196 * KB, [P, 2, AW], F32R)
        p_lo = at("p_lo", 128 * KB, [P, 2, AW], F32R)
        eb = at("eb", 200 * KB, [P, SEQ])
        c_g = [at("c_g0", 192 * KB, [P, SEQ]), at("c_g1", 196 * KB, [P, SEQ])]
        c_v = [at("c_v0", 200 * KB, [P, SEQ]), at("c_v1", 188 * KB, [P, SEQ])]
        SM = 204 * KB
        wsT = at("wsT", SM, [P, KA, P])
        v_st = at("v_st", SM, [P, 2, 2 * NKV, HD], F32R)
        ident = at("ident", SM + 2048, [P, P])
        ss = at("ss", SM + 2976, [P, NB + 1])
        ms = at("ms", SM + 2592, [P, NB])
        rs = at("rs", SM + 2624, [P, NB])
        mhalf = at("mhalf", SM + 2656, [P, NB])
        sink = at("sink", SM + 2688, [P, NH])
        nsink = at("nsink", SM + 2720, [P, NH])
        mx = at("mx", SM + 2752, [P, G])
        nm = at("nm", SM + 2784, [P, G])
        sn = at("sn", SM + 2816, [P, G])
        es = at("es", SM + 2848, [P, G])
        lsum = at("lsum", SM + 2880, [P, G])
        den = at("den", SM + 2912, [P, G])
        rden = at("rden", SM + 2944, [P, G])
        rb = at("rb", 64 * KB, [P, NH])
        brow = at("brow", 65 * KB, [P, RC + 1])
        rrow = at("rrow", 67 * KB, [P, RC + 1])

        ps = ctx.enter_context(nc.psum_tensor("ps", [P, 2, 2, HALF], F32))
        aux = ctx.enter_context(nc.psum_tensor("aux", [P, 4, HALF], F32))

        s_raw = pair("raw_loaded")
        s_wx = sem("w_out_extra_loaded")
        s_hi = sem("weight_hi_made")
        s_lo = sem("weight_lo_made")
        s_mm = sem("chunk_multiplied")
        s_free = pair("pair_evacuated")
        s_x = [sem(f"x_loaded{i}") for i in range(NB)]
        s_small = sem("smalls_loaded")
        s_gm = sem("g_mix_loaded")
        s_gs = sem("sgu_vectors_loaded")
        s_gf = sem("g_ffn_loaded")
        s_gfin = sem("g_final_loaded")
        s_conv = sem("conv_loaded")
        s_const = sem("constants_made")
        s_rrow = sem("bias_rows_ready")
        s_band = sem("band_loaded")
        s_bout = sem("bias_rows_stored")
        s_bm = sem("bias_rows_multiplied")
        s_rb = sem("bias_table_loaded")
        s_sq = sem("squares_summed")
        s_ms = sem("mean_square_ready")
        s_rs = sem("rsqrt_ready")
        s_xn = sem("block_normed")
        s_tr = sem("block_transposed")
        s_thi = sem("block_hi_made")
        s_tlo = sem("block_lo_made")
        s_vt = sem("gmlp_v_transposed")
        s_vn = sem("gmlp_v_copied")
        s_vq = sem("gmlp_v_squared")
        s_vh = sem("gmlp_v_normed")
        s_at = sem("attn_v_transposed")
        s_av = sem("attn_v_copied")
        s_sg = sem("sgu_multiplied")
        s_sb = sem("sgu_biased")
        s_yf = sem("y_a_made")
        s_yhi = sem("y_hi_made")
        s_ylo = sem("y_lo_made")
        s_st = sem("qk_hi_made")
        s_sl = sem("qk_lo_made")
        s_vst = sem("v_hi_made")
        s_vl = sem("v_lo_made")
        s_s = sem("scores_multiplied")
        s_sc = sem("scores_biased")
        s_mx = sem("row_max_ready")
        s_nm = sem("shift_ready")
        s_sn = sem("sink_shifted")
        s_e = sem("exps_ready")
        s_den = sem("denominator_ready")
        s_p = sem("probs_ready")
        s_t = sem("probs_transposed")
        s_pt = sem("probs_hi_made")
        s_pl = sem("probs_lo_made")
        s_v = sem("values_multiplied")
        s_yp = sem("y_b_part_copied")
        s_yb = sem("y_b_made")
        s_mg = sem("merged_ready")
        s_mhi = sem("merged_hi_made")
        s_mlo = sem("merged_lo_made")
        s_dhi = sem("block_hi_staged")
        s_dlo = sem("block_lo_staged")
        s_res = sem("residual_added")
        s_rx = pair("resid_loaded")
        s_c0 = sem("conv_tap2_done")
        s_c1 = sem("conv_tap1_done")
        s_si = sem("silu_done")
        s_f = sem("hidden_ready")
        s_fhi = sem("hidden_hi_made")
        s_flo = sem("hidden_lo_made")
        s_d = sem("down_multiplied")
        s_da = [sem(f"down_bank{b}_accumulated") for b in range(4)]
        s_ob = sem("output_normed")
        s_out = pair("output_stored")

        PITCH = NH * (RC + 1)
        scratch = nc.dram_tensor("band_rows", (P, NH, RC + 1), F32, kind="Internal").ap()
        band_src = bass.AP(scratch.tensor, P - 1, [[PITCH - 1, P], [RC + 1, NH], [1, 2 * P]])

        def bcast(v, n):
            return bass.AP(v.tensor, v.offset, [[0, P], [1, n]])

        def ge(eng, s, n):
            if not (isinstance(n, int) and n <= 0):
                eng.wait_ge(s, n)

        ctx.enter_context(nc.allow_non_contiguous_dma("band and broadcast loads"))
        block = ctx.enter_context(nc.Block())

        def after_first(n):
            return isinstance(n, int) and n == 1

        @block.sync
        def _(sp):
            def load(r, slot, src, cols=D):
                ge(sp, s_lo, r - 1)
                sp.dma_start(raw[:, slot, 0:cols], src).then_inc(s_raw[slot], 16)

            def load_x(n):
                sp.dma_start(xin[:, n, :], x[n]).then_inc(s_x[n], 16)

            load_x(0)
            sp.dma_start(g_bc[:, :], bcast(g_mix, D)).then_inc(s_gm, 16)
            for n in range(1, 4):
                load_x(n)
            load(0, 0, w_in[0])
            load_x(4)
            load(1, 1, w_in[1])
            for n in range(5, NB):
                load_x(n)
            sp.dma_start(rb[0:NBUCKET, :], rel_bias).then_inc(s_rb, 16)
            sp.dma_start(brow[0:NBUCKET + 1, :], bucket_rows).then_inc(s_rb, 16)
            sp.dma_start(wsT[:, :, :], w_s).then_inc(s_small, 16)
            sp.dma_start(sink[:, :], bcast(sinks, NH)).then_inc(s_small, 16)
            sp.dma_start(gs_bc[:, :], bcast(g_sgu, AW)).then_inc(s_gs, 16)
            sp.dma_start(bs_bc[:, :], bcast(b_s, AW)).then_inc(s_gs, 16)
            for slot in range(2):
                load(2 + slot, slot, w_in[2 + slot])
            sp.wait_ge(s_rrow, 1)
            sp.dma_start(scratch.rearrange("i h c -> h i c"),
                         rrow[0:NH, :].rearrange("h (o c) -> h o c", o=1).to_broadcast([NH, P, RC + 1])
                         ).then_inc(s_bout, 16)
            for slot in range(2):
                load(4 + slot, slot, w_in[4 + slot])
            sp.wait_ge(s_bout, 16)
            sp.wait_ge(s_tr, NB)
            sp.dma_start(band[:, :, :], band_src).then_inc(s_band, 16)
            with sp.Fori(3, N_IN // 2) as t:
                for slot in range(2):
                    load(2 * t + slot, slot, w_in[2 * t + slot])
            with sp.Fori(0, KD) as d:
                load(M_A + 2 * d, 0, w_in[N_IN + d])
                load(M_A + 2 * d + 1, 1, w_pa[d], KA * P)
            with sp.Fori(0, KD) as d:
                load(M_B + 2 * d, 0, w_in[N_IN + KD + d])
                load(M_B + 2 * d + 1, 1, w_pb[d], KA * P)
            load(R_O, 0, w_out[0])
            load(R_O + 1, 1, w_out[1])
            sp.wait_ge(s_sc, 2 * NB)
            sp.wait_ge(s_v, 2 * NB)
            for k in range(X_O):
                sp.dma_start(wo_raw[k], w_out[k + 2]).then_inc(s_wx, 16)
            for k in range(2 + X_O, KD):
                sp.wait_ge(s_lo, R_O + (k - 1 - X_O if k < 4 + X_O else k - 1))
                sp.dma_start(raw[:, k % 2, :], w_out[k]).then_inc(s_raw[k % 2], 16)
            sp.wait_ge(s_mm, M_O)
            for n in range(2):
                sp.dma_start(resid[:, n, :], x[n]).then_inc(s_rx[n], 16)
            sp.wait_ge(s_mlo, KD)
            sp.dma_start(g_bc[:, :], bcast(g_ffn, D)).then_inc(s_gf, 16)
            with sp.Fori(1, NB // 2) as t:
                for slot in range(2):
                    sp.wait_ge(s_res, 2 * t + slot - 1)
                    sp.dma_start(resid[:, 2 * t + slot, :], x[2 * t + slot]).then_inc(s_rx[slot], 16)
            load(R_F, 0, w_up[0])
            load(R_F + 1, 1, w_up[NF])
            sp.wait_ge(s_tr, 2 * NB)
            sp.dma_start(conv_w[:, :, :], conv).then_inc(s_conv, 16)
            sp.wait_ge(s_mm, M_F)
            sp.dma_start(gfin[:, :], bcast(g_final, D)).then_inc(s_gfin, 16)

            def ffn_tiles(i, last):
                r = R_S + 6 * i
                load(r, 0, w_up[2 * i + 1])
                load(r + 1, 1, w_up[2 * i + (NF + 1)])
                load(r + 2, 0, w_down[2 * i])
                if last:
                    load(r + 3, 1, w_down[2 * i + 1])
                    return
                load(r + 3, 1, w_up[2 * i + 2])
                load(r + 4, 0, w_down[2 * i + 1])
                load(r + 5, 1, w_up[2 * i + (NF + 2)])

            with sp.Fori(0, NPAIR - 1) as i:
                ffn_tiles(i, False)
            ffn_tiles(NPAIR - 1, True)
            for n in range(NB - 1):
                sp.wait_ge(s_ob, n + 1)
                sp.dma_start(out[n], outbuf[:, n % 2, :]).then_inc(s_out[n % 2], 16)
            for e in range(2):
                sp.wait_ge(s_ob, NB + e)
                cols = slice(e * HALF, (e + 1) * HALF)
                sp.dma_start(out[NB - 1][:, cols], outbuf[:, (NB - 1) % 2, cols]).then_inc(s_out[(NB - 1) % 2], 16)
            for slot in range(2):
                sp.wait_ge(s_out[slot], 16 * (NB // 2 + slot))

        @block.gpsimd
        def _(pool):
            pool.memset(ident[:, :], 0.0).then_inc(s_const, 1)
            pool.memset(mhalf[:, :], -0.5).then_inc(s_const, 1)
            pool.wait_ge(s_const, 2)
            pool.memset(rb[NBUCKET:NBUCKET + 1, :], 1.0).then_inc(s_const, 1)
            pool.wait_ge(s_const, 3)
            pool.affine_select(out=ident[:, :], in_=ident[:, :], compare_op=ALU.not_equal, fill=1.0, base=0,
                               pattern=[[-1, P]], channel_multiplier=1).then_inc(s_const, 1)

            def rsqrt(count, lo, hi):
                pool.wait_ge(s_ms, count)
                pool.tensor_tensor(rs[:, lo:hi], ms[:, lo:hi], mhalf[:, lo:hi], ALU.pow).then_inc(s_rs, 1)

            for n in range(NB):
                rsqrt(n + 1, n, n + 1)
            pool.wait_ge(s_small, 32)
            pool.affine_select(out=wsT[:, :, :], in_=wsT[:, :, :], compare_op=ALU.is_ge, fill=0.0, base=0,
                               pattern=[[0, KA], [1, P]], channel_multiplier=-1).then_inc(s_const, 1)
            rsqrt(NB + 1, 0, NB)
            with pool.Fori(0, NB // 2) as t:
                for j in range(2):
                    rsqrt(2 * t + (NB + 2 + j), j, j + 1)
            for n in range(NB):
                rsqrt(2 * NB + 2 + n + (n == NB - 1), n, n + 1)

        @block.scalar
        def _(act):
            def split_hi(dst, raw_slot, cols, landed):
                act.wait_ge(s_raw[raw_slot], 16 * landed)
                act.activation(dst, raw[:, raw_slot, 0:cols], ACT.Copy).then_inc(s_hi, 1)

            def tile_hi(t, slot, k=KD, landed=None):
                ge(act, s_mm, 2 * t + (slot - 1))
                split_hi(w_hi[:, slot, 0:k, :].rearrange("p k n -> p (k n)"), slot, k * P,
                         t + 1 if landed is None else landed)

            def bank_pair(j):
                return ps[:, j, :, :].rearrange("p b n -> p (b n)")

            def in_square(n):
                act.wait_ge(s_x[n], 16)
                ge(act, s_sq, n)
                act.activation(eb[:, :], xin[:, n, :], ACT.Square, accum_out=ss[:, n:n + 1]).then_inc(s_sq, 1)

            def in_hi(n):
                act.wait_ge(s_tr, n + 1)
                j = 2 * (n % 2)
                act.activation(h_hi[:, :, n * P:(n + 1) * P],
                               aux[:, j:j + 2, :].rearrange("p b (k n) -> p (b k) n", n=P),
                               ACT.Copy).then_inc(s_thi, 1)

            in_square(0)
            in_square(1)
            for n in range(NB):
                if n == NB // 2 - 1:
                    in_hi(n)
                if n + 2 < NB:
                    in_square(n + 2)
                if n in (2, 3):
                    tile_hi(0, n - 2)
                if n != NB // 2 - 1:
                    in_hi(n)

            with act.Fori(0, KA) as t:
                for j in range(2):
                    act.wait_ge(s_mm, 2 * t + (j + 1))
                    act.activation(gl[:, 2 * t + j, :], bank_pair(j), ACT.Gelu_apprx_tanh).then_inc(s_free[j], 1)
                    tile_hi(t + 1, j)
            for n in range(NB):
                act.wait_ge(s_vn, n + 1)
                act.wait_ge(s_sq, NB) if n == 0 else act.wait_ge(s_vq, n)
                act.activation(eb[:, 0:AW], vn[:, n, :], ACT.Square, accum_out=ss[:, n:n + 1]).then_inc(s_vq, 1)
            with act.Fori(KA + 1, N_IN // 2) as t:
                for j in range(2):
                    tile_hi(t, j)
            act.wait_ge(s_band, 16)
            for n in range(NB):
                if n == 4:
                    tile_hi(N_IN // 2, 0)
                act.wait_ge(s_yf, n + 1)
                act.activation(y_hi[:, :, n * P:(n + 1) * P],
                               sgu_t[:, n % 2, :].rearrange("p (c n) -> p c n", n=P), ACT.Copy).then_inc(s_yhi, 1)
            tile_hi(N_IN // 2, 1, KA)

            def stage_qk(n, g, first=False):
                ge(act, s_s, 2 * n + (g - 1))
                lo = 1 if first else 0
                keys = k_t[:, 0:P] if first else k_t[:, bass.ds(n * P - P, 2 * P)]
                rows = slice(g * HD, (g + 1) * HD)
                act.activation(q_st[rows, g, :, :], q_t[rows, :, bass.ds(n * P, P)], ACT.Copy).then_inc(s_st, 1)
                for half in range(2):
                    act.activation(k_hi[half * HD:(half + 1) * HD, g, lo:2, :].rearrange("p b n -> p (b n)"),
                                   keys[rows, :], ACT.Copy).then_inc(s_st, 1)

            def stage_v(n, first=False):
                ge(act, s_v, 2 * n)
                lo = 1 if first else 0
                vals = v_nat[:, 0:1, :] if first else v_nat[:, bass.ds(n - 1, 2), :]
                for g in range(NKV):
                    act.activation(v_st[:, lo:2, 3 * g, :], vals[:, :, g * HD:(g + 1) * HD], ACT.Copy).then_inc(s_vst, 1)

            def y_part_copy(n, g):
                act.wait_ge(s_v, 2 * n + (g + 1))
                rows, others = slice(g * HD, (g + 1) * HD), slice((1 - g) * HD, (2 - g) * HD)
                act.activation(y_part[rows, :], aux[others, 2, :], ACT.Copy).then_inc(s_yp, 1)

            def exps(j, first=False):
                act.wait_ge(s_sn, j + 1)
                cols = slice(P, 2 * P) if first else slice(0, 2 * P)
                for h in range(G):
                    act.activation(sc[:, h, cols], sc[:, h, cols], ACT.Exp, bias=nm[:, h:h + 1],
                                   accum_out=lsum[:, h:h + 1]).then_inc(s_e, 1)
                act.activation(es[:, :], sn[:, :], ACT.Exp).then_inc(s_e, 1)

            def probs_hi(j, first=False):
                act.wait_ge(s_t, j + 1)
                lo = 1 if first else 0
                act.activation(p_hi[:, lo:2, :].rearrange("p b n -> p (b n)"),
                               aux[:, 2 + lo:4, :].rearrange("p b n -> p (b n)"), ACT.Copy).then_inc(s_pt, 1)

            def gate_tanh(c):
                act.wait_ge(s_free[1], c + N_IN // 2)
                act.wait_ge(s_mm, 2 * c + (M_A + 1))
                act.activation(eb[:, :], bank_pair(0), ACT.Tanh, scale=0.5).then_inc(s_free[0], 1)

            act.wait_ge(s_free[0], N_IN // 2)
            act.wait_ge(s_free[1], N_IN // 2)
            act.wait_ge(s_av, 1)
            act.wait_ge(s_sb, NB)
            for g in range(NKV):
                stage_qk(0, g, True)

            def a_step(n, first=False, last=False):
                if not first:
                    probs_hi(2 * n - 1, after_first(n))
                    stage_qk(n, 1)
                exps(2 * n, first)
                if not first:
                    y_part_copy(n - 1, 1)
                    tile_hi(n + M_A // 2, 1, KA)
                stage_v(n, first)
                probs_hi(2 * n, first)
                if not last:
                    stage_qk(n + 1, 0)
                exps(2 * n + 1, first)
                y_part_copy(n, 0)
                gate_tanh(n)
                tile_hi(n + (M_A // 2 + 1), 0)

            a_step(0, first=True)
            a_step(1)
            with act.Fori(2, KD - 1) as n:
                a_step(n)
            a_step(KD - 1, last=True)

            probs_hi(2 * NB - 1)
            y_part_copy(NB - 1, 1)
            tile_hi(M_B // 2, 1, KA)
            act.wait_ge(s_yb, 2 * NB)
            act.wait_ge(s_mm, M_B)
            for c in range(KA):
                act.activation(y_hi[:, c, :], q_t[:, c, :], ACT.Copy).then_inc(s_yhi, 1)

            def merged_hi(d):
                act.wait_ge(s_mg, d + 1)
                act.activation(a_hi[:, d, :], mrg[:, :], ACT.Copy, scale=0.5).then_inc(s_mhi, 1)

            def b_step(d):
                gate_tanh(d + KD)
                tile_hi(d + (M_B // 2 + 1), 0)
                tile_hi(d + (M_B // 2 + 1), 1, KA)
                merged_hi(d)

            with act.Fori(0, KD - 1) as d:
                b_step(d)
            gate_tanh(2 * KD - 1)

            def w_out_hi(k):
                if 2 <= k < 2 + X_O:
                    act.wait_ge(s_wx, 16 * X_O)
                    act.activation(wo_hi[:, k, :], wo_raw[k - 2], ACT.Copy).then_inc(s_hi, 1)
                else:
                    split_hi(wo_hi[:, k, :], k % 2, D, (R_O + k - (X_O if k >= 2 else 0)) // 2 + 1)

            def block_hi(n, slot):
                ge(act, s_mm, n + (M_O - 1))
                act.activation(w_hi[:, slot, :, :], a_hi[:, :, bass.ds(n * P, P)].bitcast(F32),
                               ACT.Copy).then_inc(s_dhi, 1)

            def res_square(n, slot):
                act.wait_ge(s_res, n + 1)
                act.wait_ge(s_sq, n + NB)
                act.activation(eb[:, :], resid[:, n, :], ACT.Square, accum_out=ss[:, slot:slot + 1]).then_inc(s_sq, 1)

            def res_hi(n):
                act.wait_ge(s_tr, n + (NB + 1))
                act.activation(a_hi[:, :, bass.ds(n * P, P)],
                               aux[:, 0:2, :].rearrange("p b (k n) -> p (b k) n", n=P),
                               ACT.Copy).then_inc(s_thi, 1)

            act.wait_ge(s_mm, M_O - 1)
            for k in range(6):
                w_out_hi(k)
            merged_hi(KD - 1)
            for k in range(6, KD):
                w_out_hi(k)

            def o_step(t, first, last):
                for j in range(2):
                    n = 2 * t + j
                    res_square(n, j)
                    if not (first and j == 0):
                        res_hi(n - 1)
                    if last:
                        tile_hi(R_F // 2, j, landed=(R_F - X_O) // 2 + 1)
                    else:
                        block_hi(n + 2, j)

            o_step(0, True, False)
            with act.Fori(1, NB // 2 - 1) as t:
                o_step(t, False, False)
            o_step(NB // 2 - 1, False, True)
            res_hi(NB - 1)

            def conv_tap2(i, c):
                p = c // 2
                chunk = 2 * i + p if c % 2 == 0 else 2 * i + (NF + p)
                act.wait_ge(s_mm, 4 * i + (M_F + c + 1))
                ge(act, s_flo, 2 * i + (p - 1))
                act.activation((c_v if c % 2 else c_g)[p][:, :], bank_pair(c % 2), ACT.Identity,
                               bias=conv_w[:, chunk, 3:4], scale=conv_w[:, chunk, 2:3]).then_inc(s_c0, 1)

            def silu(i, p):
                act.wait_ge(s_free[0], 2 * i + (F_O + p + 1))
                act.activation(c_g[p][:, :], c_g[p][:, :], ACT.Silu).then_inc(s_si, 1)

            def hidden_hi(i, p, last=False):
                act.wait_ge(s_f, 2 * i + (p + 1))
                act.activation((fl_hi if last else f_hi)[:, p, :], c_g[p][:, :], ACT.Copy).then_inc(s_fhi, 1)

            def ffn_up_hi(i, j, slot):
                split_hi(w_hi[:, slot, :, :].rearrange("p k n -> p (k n)"), j % 2, D, 3 * i + (R_S + j - X_O) // 2 + 1)

            def ffn_down_hi(i, j, p, last=False):
                if last:
                    act.wait_ge(s_mm, M_F + 4 * NPAIR)
                else:
                    ge(act, s_d, 2 * NB * i)
                split_hi((wdl_hi if last else wd_hi)[:, p, :], j % 2, D, 3 * i + (R_S + j - X_O) // 2 + 1)

            def ffn_step(i, last=False):
                conv_tap2(i, 0)
                ffn_up_hi(i, 0, 0)
                silu(i, 0)
                conv_tap2(i, 1)
                ffn_up_hi(i, 1, 1)
                if not last:
                    ffn_down_hi(i, 2, 0)
                hidden_hi(i, 0, last)
                conv_tap2(i, 2)
                if not last:
                    ffn_up_hi(i, 3, 0)
                    ffn_down_hi(i, 4, 1)
                silu(i, 1)
                conv_tap2(i, 3)
                if not last:
                    ffn_up_hi(i, 5, 1)
                    hidden_hi(i, 1)
                else:
                    ffn_down_hi(i, 2, 0, True)
                    hidden_hi(i, 1, True)
                    ffn_down_hi(i, 3, 1, True)

            act.wait_ge(s_conv, 16)
            ffn_step(0)
            with act.Fori(1, NPAIR - 1) as i:
                ffn_step(i)
            ffn_step(NPAIR - 1, last=True)
            def out_square(count, col, src):
                act.wait_ge(s_sq, count)
                act.activation(c_v[0][:, 0:src.shape[-1]], src, ACT.Square, accum_out=ss[:, col:col + 1]).then_inc(s_sq, 1)

            for n in range(NB - 1):
                for q in (2 * n, 2 * n + 1):
                    act.wait_ge(s_da[q % 4], 4 * (NPAIR - 1) + q // 4 + 2)
                out_square(2 * NB + n, n, resid[:, n, :])
            for e in range(2):
                act.wait_ge(s_da[2 + e], 4 * NPAIR + 1)
                out_square(3 * NB - 1 + e, NB - 1 + e, resid[:, NB - 1, e * HALF:(e + 1) * HALF])

        @block.vector
        def _(dve):
            def split_lo(dst, hi, src, made):
                dve.wait_ge(s_hi, made)
                dve.tensor_tensor(dst, src, hi.bitcast(F32), ALU.subtract).then_inc(s_lo, 1)

            def tile_lo(t, slot, k=KD):
                split_lo(w_lo[:, slot, 0:k, :].rearrange("p k n -> p (k n)"),
                         w_hi[:, slot, 0:k, :].rearrange("p k n -> p (k n)"),
                         raw[:, slot, 0:k * P], 2 * t + (slot + 1))

            def bank_pair(j):
                return ps[:, j, :, :].rearrange("p b n -> p (b n)")

            def mean_square(col, cols, width, s, count):
                dve.wait_ge(s, count)
                dve.tensor_scalar(ms[:, col:col + cols], ss[:, col:col + cols], 1.0 / width, EPS,
                                  ALU.mult, ALU.add).then_inc(s_ms, 1)

            def in_norm(n):
                dve.wait_ge(s_rs, n + 1)
                ge(dve, s_tr, n - 1)
                dve.scalar_tensor_tensor(out=xn2[:, n % 2, :], in0=xin[:, n, :], scalar=rs[:, n:n + 1],
                                         in1=g_bc[:, :], op0=ALU.mult, op1=ALU.mult).then_inc(s_xn, 1)

            def in_lo(n):
                dve.wait_ge(s_thi, n + 1)
                j = 2 * (n % 2)
                dve.tensor_tensor(h_lo[:, :, n * P:(n + 1) * P],
                                  aux[:, j:j + 2, :].rearrange("p b (k n) -> p (b k) n", n=P),
                                  h_hi[:, :, n * P:(n + 1) * P].bitcast(F32), ALU.subtract).then_inc(s_tlo, 1)

            mean_square(0, 1, D, s_sq, 1)
            dve.wait_ge(s_gm, 16)
            in_norm(0)
            mean_square(1, 1, D, s_sq, 2)
            for n in range(1, NB):
                in_norm(n)
                if n + 1 < NB:
                    mean_square(n + 1, 1, D, s_sq, n + 2)
                if n == 3:
                    tile_lo(0, 0)
                if n == 4:
                    tile_lo(0, 1)
                else:
                    in_lo(n - 1)
                if n == 3:
                    in_lo(3)
            in_lo(NB - 1)
            dve.wait_ge(s_bm, 1)
            dve.tensor_copy(rrow[0:NH, 0:RC], ps[0:NH, 1, 1, 0:RC])
            dve.memset(rrow[0:NH, RC:RC + 1], 0.0).then_inc(s_rrow, 1)
            with dve.Fori(1, KA) as t:
                for j in range(2):
                    tile_lo(t, j)

            def v_out(ns):
                for n in ns:
                    dve.wait_ge(s_vt, n + 1)
                    dve.tensor_copy(vn[:, n, :], aux[:, n % 4, :]).then_inc(s_vn, 1)

            v_out(range(4))
            for j in range(2):
                tile_lo(KA, j)
            v_out(range(4, NB))
            mean_square(0, NB, AW, s_vq, NB)
            dve.wait_ge(s_rs, NB + 1)
            dve.wait_ge(s_gs, 32)
            for n in range(NB):
                dve.scalar_tensor_tensor(out=vn[:, n, :], in0=vn[:, n, :], scalar=rs[:, n:n + 1],
                                         in1=gs_bc[:, :], op0=ALU.mult, op1=ALU.mult).then_inc(s_vh, 1)

            def qkv_out(t, j):
                dve.wait_ge(s_mm, 2 * t + (j + 1))
                dve.tensor_copy(qkv[:, 2 * t + (j - 2 * KA), :], bank_pair(j)).then_inc(s_free[j], 1)

            for j in range(2):
                qkv_out(KA, j)
                tile_lo(KA + 1, j)
            dve.wait_ge(s_at, 1)
            dve.tensor_copy(v_nat[:, :, :].rearrange("p b n -> p (b n)"),
                            aux[:, 0:2, :].rearrange("p b n -> p (b n)")).then_inc(s_av, 1)
            for j in range(2):
                qkv_out(KA + 1, j)
                tile_lo(KA + 2, j)

            def y_a_lo(n):
                dve.wait_ge(s_yhi, n + 1)
                dve.tensor_tensor(y_lo[:, :, n * P:(n + 1) * P],
                                  sgu_t[:, n % 2, :].rearrange("p (c n) -> p c n", n=P),
                                  y_hi[:, :, n * P:(n + 1) * P].bitcast(F32), ALU.subtract).then_inc(s_ylo, 1)

            def y_a(n):
                dve.wait_ge(s_sg, n + 1)
                ge(dve, s_ylo, n - 1)
                dve.tensor_tensor(sgu_t[:, n % 2, :], aux[:, n % 4, :], bs_bc[:, :], ALU.add).then_inc(s_sb, 1)
                if n >= 1:
                    y_a_lo(n - 1)
                t3 = sgu_t[:, n % 2, :].rearrange("p (c n) -> p c n", n=P)
                dve.wait_ge(s_sb, n + 1)
                dve.tensor_tensor(t3, t3, u_t[:, :, n * P:(n + 1) * P], ALU.mult).then_inc(s_yf, 1)

            for n in range(4):
                y_a(n)
            qkv_out(N_IN // 2 - 1, 0)
            tile_lo(N_IN // 2, 0)
            for n in range(4, NB):
                y_a(n)
            y_a_lo(NB - 1)
            qkv_out(N_IN // 2 - 1, 1)
            tile_lo(N_IN // 2, 1, KA)
            dve.wait_ge(s_small, 32)
            dve.tensor_scalar(nsink[:, :], sink[:, :], -1.0, None, ALU.mult).then_inc(s_const, 1)

            def stage_qk_lo(n, g, first=False):
                dve.wait_ge(s_st, 6 * n + (3 * g + 3))
                lo = 1 if first else 0
                keys = k_t[:, 0:P] if first else k_t[:, bass.ds(n * P - P, 2 * P)]
                rows, others = slice(g * HD, (g + 1) * HD), slice((1 - g) * HD, (2 - g) * HD)
                dve.tensor_tensor(q_st[others, g, :, :], q_t[rows, :, bass.ds(n * P, P)],
                                  q_st[rows, g, :, :].bitcast(F32), ALU.subtract).then_inc(s_sl, 1)
                dve.tensor_tensor(k_lo[rows, lo:2, :].rearrange("p b n -> p (b n)"), keys[rows, :],
                                  k_hi[rows, g, lo:2, :].rearrange("p b n -> p (b n)").bitcast(F32),
                                  ALU.subtract).then_inc(s_sl, 1)

            def stage_v_lo(n, first=False):
                dve.wait_ge(s_vst, 2 * n + 2)
                lo = 1 if first else 0
                vals = v_nat[:, 0:1, :] if first else v_nat[:, bass.ds(n - 1, 2), :]
                for g in range(NKV):
                    dve.tensor_tensor(v_st[:, lo:2, 1 + g, :], vals[:, :, g * HD:(g + 1) * HD],
                                      v_st[:, lo:2, 3 * g, :].bitcast(F32), ALU.subtract).then_inc(s_vl, 1)

            def probs_lo(j, first=False):
                dve.wait_ge(s_pt, j + 1)
                lo = 1 if first else 0
                dve.tensor_tensor(p_lo[:, lo:2, :].rearrange("p b n -> p (b n)"),
                                  aux[:, 2 + lo:4, :].rearrange("p b n -> p (b n)"),
                                  p_hi[:, lo:2, :].rearrange("p b n -> p (b n)").bitcast(F32),
                                  ALU.subtract).then_inc(s_pl, 1)

            def softmax(n, g, first):
                j = 2 * n + g
                lo = P if first else 0
                s4 = sc[:, :, lo:2 * P]
                dve.wait_ge(s_s, j + 1)
                raw_scores = aux[:, 0:2, :].rearrange("p b (h k) -> p (b h) k", k=2 * P)
                dve.scalar_tensor_tensor(out=s4, in0=raw_scores[:, :, lo:2 * P], scalar=SCALE, in1=band[:, g * G:(g + 1) * G, lo:2 * P],
                                         op0=ALU.mult, op1=ALU.add).then_inc(s_sc, 1)
                dve.wait_ge(s_sc, j + 1)
                dve.tensor_reduce(mx[:, :], s4, AX_X, ALU.max).then_inc(s_mx, 1)
                dve.wait_ge(s_mx, j + 1)
                dve.scalar_tensor_tensor(out=nm[:, :], in0=mx[:, :], scalar=-1.0, in1=nsink[:, g * G:(g + 1) * G],
                                         op0=ALU.mult, op1=ALU.min).then_inc(s_nm, 1)
                dve.wait_ge(s_nm, j + 1)
                dve.tensor_tensor(sn[:, :], sink[:, g * G:(g + 1) * G], nm[:, :], ALU.add).then_inc(s_sn, 1)

            def normalise(n, g, first):
                j = 2 * n + g
                lo = P if first else 0
                dve.wait_ge(s_e, (G + 1) * j + (G + 1))
                dve.tensor_tensor(den[:, :], lsum[:, :], es[:, :], ALU.add).then_inc(s_den, 1)
                dve.wait_ge(s_den, 2 * j + 1)
                dve.reciprocal(rden[:, :], den[:, :]).then_inc(s_den, 1)
                dve.wait_ge(s_den, 2 * j + 2)
                for h in range(G):
                    dve.tensor_scalar(sc[:, h, lo:2 * P], sc[:, h, lo:2 * P], rden[:, h:h + 1], None,
                                      ALU.mult).then_inc(s_p, 1)

            def y_b(n, g):
                dve.wait_ge(s_yp, 2 * n + (g + 1))
                rows = slice(g * HD, (g + 1) * HD)
                dve.tensor_tensor(q_t[rows, :, bass.ds(n * P, P)],
                                  aux[rows, 2, :].rearrange("p (c n) -> p c n", n=P),
                                  y_part[rows, :].rearrange("p (c n) -> p c n", n=P), ALU.add).then_inc(s_yb, 1)

            def a_step(n, first=False, last=False):
                softmax(n, 0, first)
                if not first:
                    probs_lo(2 * n - 1, after_first(n))
                    stage_qk_lo(n, 1)
                normalise(n, 0, first)
                if not first:
                    y_b(n - 1, 1)
                    tile_lo(n + M_A // 2, 1, KA)
                stage_v_lo(n, first)
                softmax(n, 1, first)
                probs_lo(2 * n, first)
                if not last:
                    stage_qk_lo(n + 1, 0)
                normalise(n, 1, first)
                y_b(n, 0)
                tile_lo(n + (M_A // 2 + 1), 0)
                dve.wait_ge(s_mm, 2 * n + (M_A + 2))
                dve.wait_ge(s_free[0], n + (N_IN // 2 + 1))
                dve.scalar_tensor_tensor(out=half_m[:, n, :], in0=eb[:, :], scalar=1.0, in1=bank_pair(1),
                                         op0=ALU.add, op1=ALU.mult).then_inc(s_free[1], 1)

            dve.wait_ge(s_band, 16)
            dve.wait_ge(s_const, 6)
            for g in range(NKV):
                stage_qk_lo(0, g, True)
            a_step(0, first=True)
            a_step(1)
            with dve.Fori(2, KD - 1) as n:
                a_step(n)
            a_step(KD - 1, last=True)

            probs_lo(2 * NB - 1)
            y_b(NB - 1, 1)
            tile_lo(M_B // 2, 1, KA)
            for c in range(KA):
                dve.wait_ge(s_yhi, NB + c + 1)
                dve.tensor_tensor(y_lo[:, c, :], q_t[:, c, :], y_hi[:, c, :].bitcast(F32),
                                  ALU.subtract).then_inc(s_ylo, 1)

            def b_merge(d):
                dve.wait_ge(s_mm, 2 * d + (M_B + 2))
                dve.wait_ge(s_free[0], d + (M_B // 2 + 1))
                ge(dve, s_mlo, d)
                dve.scalar_tensor_tensor(out=mrg[:, :], in0=eb[:, :], scalar=1.0, in1=bank_pair(1),
                                         op0=ALU.add, op1=ALU.mult).then_inc(s_free[1], 1)
                dve.wait_ge(s_free[1], d + (M_B // 2 + 1))
                dve.tensor_tensor(mrg[:, :], mrg[:, :], half_m[:, d, :], ALU.add).then_inc(s_mg, 1)

            def merged_lo(d):
                dve.wait_ge(s_mhi, d + 1)
                dve.scalar_tensor_tensor(out=a_lo[:, d, :], in0=mrg[:, :], scalar=0.5,
                                         in1=a_hi[:, d, :].bitcast(F32),
                                         op0=ALU.mult, op1=ALU.subtract).then_inc(s_mlo, 1)

            def b_step(d):
                tile_lo(d + (M_B // 2 + 1), 0)
                b_merge(d)
                tile_lo(d + (M_B // 2 + 1), 1, KA)
                merged_lo(d)

            b_step(0)
            with dve.Fori(1, KD - 1) as d:
                b_step(d)

            def w_out_lo(k):
                split_lo(wo_lo[:, k, :], wo_hi[:, k, :], wo_raw[k - 2] if 2 <= k < 2 + X_O else raw[:, k % 2, :],
                         R_O + k + 1)

            def block_lo(n, slot):
                dve.wait_ge(s_dhi, n - 1)
                dve.tensor_copy(w_lo[:, slot, :, :], a_lo[:, :, bass.ds(n * P, P)].bitcast(F32)).then_inc(s_dlo, 1)

            def residual(n, j):
                dve.wait_ge(s_mm, n + (M_O + 1))
                dve.wait_ge(s_rx[j], (n - j) * 8 + 16)
                dve.tensor_tensor(resid[:, n, :], bank_pair(j), resid[:, n, :], ALU.add).then_inc(s_res, 1)
                dve.wait_ge(s_res, n + 1)

            def res_norm(n, j):
                dve.wait_ge(s_rs, n + (NB + 2))
                dve.wait_ge(s_tr, n + (NB - 1))
                dve.scalar_tensor_tensor(out=xn2[:, j, :], in0=resid[:, n, :], scalar=rs[:, j:j + 1],
                                         in1=g_bc[:, :], op0=ALU.mult, op1=ALU.mult).then_inc(s_xn, 1)

            def res_lo(n):
                dve.wait_ge(s_thi, n + (NB + 1))
                dve.tensor_tensor(a_lo[:, :, bass.ds(n * P, P)],
                                  aux[:, 0:2, :].rearrange("p b (k n) -> p (b k) n", n=P),
                                  a_hi[:, :, bass.ds(n * P, P)].bitcast(F32), ALU.subtract).then_inc(s_tlo, 1)

            for k in range(4):
                w_out_lo(k)
            b_merge(KD - 1)
            for k in range(4, 6):
                w_out_lo(k)
            dve.wait_ge(s_lo, R_O + 6)
            merged_lo(KD - 1)
            for k in range(6, KD):
                w_out_lo(k)
            dve.wait_ge(s_gf, 16)

            def o_step(t, first, last):
                for j in range(2):
                    n = 2 * t + j
                    residual(n, j)
                    dve.wait_ge(s_sq, n + (NB + 1))
                    mean_square(j, 1, D, s_sq, n + (NB + 1))
                    if not (first and j == 0):
                        res_lo(n - 1)
                    if last:
                        tile_lo(R_F // 2, j)
                    else:
                        block_lo(n + 2, j)
                    res_norm(n, j)

            o_step(0, True, False)
            with dve.Fori(1, NB // 2 - 1) as t:
                o_step(t, False, False)
            o_step(NB // 2 - 1, False, True)
            res_lo(NB - 1)

            def accumulate(i, q):
                dve.wait_ge(s_d, 2 * NB * i + (q + 1))
                r = resid[:, q // 2, (q % 2) * HALF:(q % 2 + 1) * HALF]
                dve.tensor_tensor(r, aux[:, q % 4, :], r, ALU.add).then_inc(s_da[q % 4], 1)

            def conv_taps(i, c, between=None):
                p = c // 2
                chunk = 2 * i + p if c % 2 == 0 else 2 * i + (NF + p)
                buf = (c_v if c % 2 else c_g)[p]
                dve.wait_ge(s_c0, 4 * i + (c + 1))
                dve.scalar_tensor_tensor(out=buf[:, 1:SEQ], in0=bank_pair(c % 2)[:, 0:SEQ - 1],
                                         scalar=conv_w[:, chunk, 1:2], in1=buf[:, 1:SEQ],
                                         op0=ALU.mult, op1=ALU.add).then_inc(s_c1, 1)
                if between is not None:
                    accumulate(i - 1, between)
                dve.wait_ge(s_c1, 4 * i + (c + 1))
                dve.scalar_tensor_tensor(out=buf[:, 2:SEQ], in0=bank_pair(c % 2)[:, 0:SEQ - 2],
                                         scalar=conv_w[:, chunk, 0:1], in1=buf[:, 2:SEQ],
                                         op0=ALU.mult, op1=ALU.add).then_inc(s_free[c % 2], 1)

            def hidden(i, p):
                dve.wait_ge(s_free[1], 2 * i + (F_O + p + 1))
                dve.wait_ge(s_si, 2 * i + (p + 1))
                dve.tensor_tensor(c_g[p][:, :], c_g[p][:, :], c_v[p][:, :], ALU.mult).then_inc(s_f, 1)

            def hidden_lo(i, p, last=False):
                dve.wait_ge(s_fhi, 2 * i + (p + 1))
                lo, hi = (fl_lo, fl_hi) if last else (f_lo, f_hi)
                dve.tensor_tensor(lo[:, p, :], c_g[p][:, :], hi[:, p, :].bitcast(F32),
                                  ALU.subtract).then_inc(s_flo, 1)

            def ffn_up_lo(i, j, slot):
                split_lo(w_lo[:, slot, :, :].rearrange("p k n -> p (k n)"),
                         w_hi[:, slot, :, :].rearrange("p k n -> p (k n)"), raw[:, j % 2, :], 6 * i + (R_S + j + 1))

            def ffn_down_lo(i, j, p, last=False):
                lo, hi = (wdl_lo, wdl_hi) if last else (wd_lo, wd_hi)
                split_lo(lo[:, p, :], hi[:, p, :], raw[:, j % 2, :], 6 * i + (R_S + j + 1))

            def ffn_step(i, first=False, last=False):
                if first or last:
                    conv_taps(i, 0)
                    ffn_up_lo(i, 0, 0)
                else:
                    conv_taps(i, 0, 0)
                    for q in range(1, 4):
                        accumulate(i - 1, q)
                    ffn_up_lo(i, 0, 0)
                    for q in range(4, 2 * NB):
                        accumulate(i - 1, q)
                conv_taps(i, 1)
                hidden(i, 0)
                ffn_up_lo(i, 1, 1)
                if not last:
                    ffn_down_lo(i, 2, 0)
                hidden_lo(i, 0, last)
                conv_taps(i, 2)
                if not last:
                    ffn_up_lo(i, 3, 0)
                    ffn_down_lo(i, 4, 1)
                    conv_taps(i, 3)
                    hidden(i, 1)
                    ffn_up_lo(i, 5, 1)
                    hidden_lo(i, 1)
                else:
                    conv_taps(i, 3, 0)
                    accumulate(i - 1, 1)
                    hidden(i, 1)
                    accumulate(i - 1, 2)
                    accumulate(i - 1, 3)
                    ffn_down_lo(i, 2, 0, True)
                    accumulate(i - 1, 4)
                    accumulate(i - 1, 5)
                    hidden_lo(i, 1, True)
                    accumulate(i - 1, 6)
                    accumulate(i - 1, 7)
                    ffn_down_lo(i, 3, 1, True)
                    for q in range(8, 2 * NB):
                        accumulate(i - 1, q)

            for b in range(4):
                dve.sem_inc(s_da[b], 1)
            ffn_step(0, first=True)
            with dve.Fori(1, NPAIR - 1) as i:
                ffn_step(i)
            ffn_step(NPAIR - 1, last=True)

            def out_norm(n, e_cols):
                dve.scalar_tensor_tensor(out=outbuf[:, n % 2, e_cols], in0=resid[:, n, e_cols], scalar=rs[:, n:n + 1],
                                         in1=gfin[:, e_cols], op0=ALU.mult, op1=ALU.mult).then_inc(s_ob, 1)

            dve.wait_ge(s_gfin, 16)
            for n in range(NB):
                accumulate(NPAIR - 1, 2 * n)
                if n >= 1:
                    mean_square(n - 1, 1, D, s_sq, 2 * NB + n)
                accumulate(NPAIR - 1, 2 * n + 1)
                if n >= 1:
                    dve.wait_ge(s_rs, 2 * NB + n + 1)
                    ge(dve, s_out[(n - 1) % 2], 16 * ((n - 1) // 2))
                    out_norm(n - 1, slice(0, D))
            last = NB - 1
            mean_square(last, 1, D, s_sq, 3 * NB)
            dve.wait_ge(s_sq, 3 * NB + 1)
            dve.wait_ge(s_ms, 3 * NB + 1)
            dve.scalar_tensor_tensor(out=ms[:, last:last + 1], in0=ss[:, NB:NB + 1], scalar=1.0 / D,
                                     in1=ms[:, last:last + 1], op0=ALU.mult, op1=ALU.add).then_inc(s_ms, 1)
            dve.wait_ge(s_rs, 3 * NB + 1)
            dve.wait_ge(s_out[last % 2], 16 * (last // 2))
            for e in range(2):
                out_norm(last, slice(e * HALF, (e + 1) * HALF))

        @block.tensor
        def _(pe):
            def product(dst, s_hi_ap, s_lo_ap, m_hi, m_lo, first, last):
                pe.matmul(dst, s_lo_ap, m_hi, start=first, stop=False)
                pe.matmul(dst, s_hi_ap, m_lo, start=False, stop=False)
                return pe.matmul(dst, s_hi_ap, m_hi, start=False, stop=last)

            def chunk_part(slot, acts_hi, acts_lo, kn, half, ks, lo=0, hi=HALF):
                cols = slice(half * HALF + lo, half * HALF + hi)
                for k in ks:
                    mm = product(ps[:, slot, half, lo:hi], w_hi[:, slot, k, :], w_lo[:, slot, k, :],
                                 acts_hi[:, k, cols], acts_lo[:, k, cols], k == 0, k == kn - 1)
                return mm

            def chunk(slot, acts_hi, acts_lo, kn=KD):
                for half in range(2):
                    mm = chunk_part(slot, acts_hi, acts_lo, kn, half, range(kn))
                mm.then_inc(s_mm, 1)

            def ready(r, slot, freed):
                pe.wait_ge(s_lo, r + 1)
                pe.wait_ge(s_free[slot], freed)

            def transposes(src, pairs):
                for k in range(KD):
                    mm = pe.transpose(aux[:, pairs + k // 4, (k % 4) * P:(k % 4 + 1) * P],
                                      src[:, k * P:(k + 1) * P], ident[:, :])
                mm.then_inc(s_tr, 1)

            def in_transpose(n, j):
                pe.wait_ge(s_xn, n + 1)
                ge(pe, s_tlo, n - 1)
                transposes(xn2[:, j, :], 2 * j)

            pe.wait_ge(s_const, 4)
            for n in range(NB // 2):
                in_transpose(n, n % 2)

            def in_pair(t):
                for j in range(2):
                    pe.wait_ge(s_lo, 2 * t + (j + 1))
                    ge(pe, s_free[j], t)
                    chunk(j, h_hi, h_lo)

            pe.wait_ge(s_lo, 1)
            pe.wait_ge(s_tlo, 2)
            chunk_part(0, h_hi, h_lo, KD, 0, range(KD), hi=2 * P)
            in_transpose(4, 0)
            pe.wait_ge(s_tlo, 4)
            chunk_part(0, h_hi, h_lo, KD, 0, range(KD), lo=2 * P)
            in_transpose(5, 1)
            pe.wait_ge(s_lo, 2)
            chunk_part(1, h_hi, h_lo, KD, 0, range(4))
            in_transpose(6, 0)
            chunk_part(1, h_hi, h_lo, KD, 0, range(4, 6))
            in_transpose(7, 1)
            pe.wait_ge(s_rb, 32)
            pe.matmul(ps[0:NH, 1, 1, 0:RC], rb[0:NBUCKET + 1, :], brow[0:NBUCKET + 1, 0:RC],
                      start=True, stop=True).then_inc(s_bm, 1)
            chunk_part(1, h_hi, h_lo, KD, 0, range(6, KD))
            pe.wait_ge(s_tlo, NB)
            chunk_part(0, h_hi, h_lo, KD, 1, range(KD)).then_inc(s_mm, 1)
            pe.wait_ge(s_rrow, 1)
            chunk_part(1, h_hi, h_lo, KD, 1, range(KD)).then_inc(s_mm, 1)

            def v_transposes(ns):
                for n in ns:
                    ge(pe, s_vn, n - 3)
                    for c in range(KA):
                        mm = pe.transpose(aux[:, n % 4, c * P:(c + 1) * P], gl[:, c, n * P:(n + 1) * P], ident[:, :])
                    mm.then_inc(s_vt, 1)

            with pe.Fori(1, KA - 1) as t:
                in_pair(t)
            for j in range(2):
                pe.wait_ge(s_free[j], 2)
            v_transposes(range(4))
            in_pair(KA - 1)
            v_transposes(range(4, NB))
            in_pair(KA)
            pe.wait_ge(s_vn, NB)
            pe.wait_ge(s_free[0], KA + 1)
            for n in range(NB):
                mm = pe.transpose(aux[:, n // 4, (n % 4) * P:(n % 4 + 1) * P], v_t[:, n * P:(n + 1) * P], ident[:, :])
            mm.then_inc(s_at, 1)
            in_pair(KA + 1)

            def spatial(ns):
                for n in ns:
                    pe.wait_ge(s_vh, n + 1)
                    ge(pe, s_sb, n - 3)
                    for g in range(KA):
                        mm = pe.matmul(aux[:, n % 4, g * P:(g + 1) * P], vn[:, n, g * P:(g + 1) * P],
                                       wsT[:, g, :], start=True, stop=True)
                    mm.then_inc(s_sg, 1)

            pe.wait_ge(s_const, 5)
            pe.wait_ge(s_av, 1)
            spatial(range(4))
            for j in range(2):
                pe.wait_ge(s_lo, N_IN - 1 + j)
                pe.wait_ge(s_free[j], N_IN // 2 - 1)
                chunk(j, h_hi, h_lo)
                if j == 0:
                    spatial(range(4, NB))

            def scores(n, g, first=False):
                j = 2 * n + g
                pe.wait_ge(s_sl, 4 * n + (2 * g + 2))
                ge(pe, s_sc, j)
                rows = slice(g * HD, (g + 1) * HD)
                lo = 1 if first else 0
                for h in range(G):
                    dst = aux[:, h // 2, (h % 2) * 2 * P + lo * P:(h % 2 + 1) * 2 * P]
                    pe.matmul(dst, q_st[rows, g, h, :], k_lo[rows, lo:2, :].rearrange("p b n -> p (b n)"),
                              start=True, stop=False)
                    mm = pe.matmul(dst, q_st[:, g, h, :], k_hi[:, g, lo:2, :].rearrange("p b n -> p (b n)"),
                                   start=False, stop=True)
                mm.then_inc(s_s, 1)

            def probs_t(n, g, first=False):
                j = 2 * n + g
                pe.wait_ge(s_p, G * j + G)
                ge(pe, s_yb, j)
                for b in range(1 if first else 0, 2):
                    for h in range(G):
                        mm = pe.transpose(aux[:, 2 + b, h * P:(h + 1) * P], sc[:, h, b * P:(b + 1) * P], ident[:, :])
                mm.then_inc(s_t, 1)

            def values(n, g, first=False):
                j = 2 * n + g
                pe.wait_ge(s_vl, 2 * n + 2)
                pe.wait_ge(s_pl, j + 1)
                lo = 1 if first else 0
                for b in range(lo, 2):
                    both = v_st[:, b, 2 * g:2 * g + 2, :].rearrange("p a n -> p (a n)")
                    pe.matmul(aux[:, 2, :], both, p_lo[:, b, :], start=b == lo, stop=False)
                    mm = pe.matmul(aux[:, 2, :], both, p_hi[:, b, :], start=False, stop=b == 1)
                mm.then_inc(s_v, 1)

            def a_step(n, first=False):
                cut = 7 if first else 4
                if first:
                    ready(2 * n + M_A, 0, n + M_A // 2)
                    chunk_part(0, h_hi, h_lo, KD, 0, range(0, 6))
                    pe.wait_ge(s_sb, NB)
                    scores(n, 0, first)
                    chunk_part(0, h_hi, h_lo, KD, 0, range(6, KD))
                else:
                    probs_t(n - 1, 1, after_first(n))
                    scores(n, 0)
                    ready(2 * n + M_A, 0, n + M_A // 2)
                    chunk_part(0, h_hi, h_lo, KD, 0, range(KD))
                    values(n - 1, 1, after_first(n))
                chunk_part(0, h_hi, h_lo, KD, 1, range(cut))
                probs_t(n, 0, first)
                scores(n, 1, first)
                chunk_part(0, h_hi, h_lo, KD, 1, range(cut, KD)).then_inc(s_mm, 1)
                ready(2 * n + (M_A + 1), 1, n + M_A // 2)
                if first:
                    pe.wait_ge(s_ylo, NB)
                chunk_part(1, y_hi, y_lo, KA, 0, range(KA))
                values(n, 0, first)
                chunk_part(1, y_hi, y_lo, KA, 1, range(KA)).then_inc(s_mm, 1)

            a_step(0, first=True)
            a_step(1)
            with pe.Fori(2, KD) as n:
                a_step(n)

            probs_t(NB - 1, 1)
            ready(M_B, 0, M_B // 2)
            chunk_part(0, h_hi, h_lo, KD, 0, range(0, 4))
            values(NB - 1, 1)
            chunk_part(0, h_hi, h_lo, KD, 0, range(4, 8))
            chunk_part(0, h_hi, h_lo, KD, 1, range(0, 8)).then_inc(s_mm, 1)
            pe.wait_ge(s_ylo, NB + KA)
            ready(M_B + 1, 1, M_B // 2)
            chunk(1, y_hi, y_lo, KA)
            with pe.Fori(1, KD) as d:
                ready(2 * d + M_B, 0, d + M_B // 2)
                chunk(0, h_hi, h_lo)
                ready(2 * d + (M_B + 1), 1, d + M_B // 2)
                chunk(1, y_hi, y_lo, KA)

            def out_part(j, k, hi, lo):
                for e in range(2):
                    cols = slice(e * HALF, (e + 1) * HALF)
                    mm = product(ps[:, j, e, :], hi, lo, wo_hi[:, k, cols], wo_lo[:, k, cols], k == 0, k == KD - 1)
                return mm

            def out_first(n, ks):
                for k in ks:
                    pe.wait_ge(s_lo, R_O + k + 1)
                    pe.wait_ge(s_mlo, KD if k == KD - 1 else KD - 1)
                    mm = out_part(n, k, a_hi[:, k, n * P:(n + 1) * P], a_lo[:, k, n * P:(n + 1) * P])
                return mm

            def out_block(n, j):
                pe.wait_ge(s_dlo, n - 1)
                pe.wait_ge(s_res, n - 1)
                for k in range(KD):
                    mm = out_part(j, k, w_hi[:, j, k, :], w_lo[:, j, k, :])
                mm.then_inc(s_mm, 1)

            def res_transpose(n, j):
                pe.wait_ge(s_xn, n + (NB + 1))
                pe.wait_ge(s_tlo, n + NB)
                transposes(xn2[:, j, :], 0)

            pe.wait_ge(s_free[0], F_O)
            out_first(0, range(KD - 2))
            pe.wait_ge(s_free[1], F_O)
            out_first(1, range(2))
            out_first(0, range(KD - 2, KD)).then_inc(s_mm, 1)
            out_first(1, range(2, KD)).then_inc(s_mm, 1)
            res_transpose(0, 0)
            with pe.Fori(1, NB // 2) as t:
                out_block(2 * t, 0)
                res_transpose(2 * t - 1, 1)
                out_block(2 * t + 1, 1)
                res_transpose(2 * t, 0)

            def up(i, c, r):
                pe.wait_ge(s_lo, r + 1)
                pe.wait_ge(s_free[c % 2], 2 * i + (F_O + c // 2))
                chunk(c % 2, a_hi, a_lo)

            def down(i, made, fh, fl, wh, wl):
                pe.wait_ge(s_lo, made)
                pe.wait_ge(s_flo, 2 * i + 2)
                for q in range(2 * NB):
                    n, e = q // 2, q % 2
                    pe.wait_ge(s_da[q % 4], 4 * i + (q // 4 + 1))
                    for p in range(2):
                        mm = product(aux[:, q % 4, :], fh[:, p, n * P:(n + 1) * P], fl[:, p, n * P:(n + 1) * P],
                                     wh[:, p, e * HALF:(e + 1) * HALF], wl[:, p, e * HALF:(e + 1) * HALF],
                                     p == 0, p == 1)
                    mm.then_inc(s_d, 1)

            pe.wait_ge(s_lo, R_F + 1)
            pe.wait_ge(s_res, NB - 1)
            pe.wait_ge(s_tlo, NB + NB // 2)
            chunk_part(0, a_hi, a_lo, KD, 0, range(KD))
            pe.wait_ge(s_lo, R_F + 2)
            pe.wait_ge(s_res, NB)
            chunk_part(1, a_hi, a_lo, KD, 0, range(0, 4))
            res_transpose(NB - 1, 1)
            chunk_part(1, a_hi, a_lo, KD, 0, range(4, KD))
            pe.wait_ge(s_tlo, 2 * NB)
            for j in range(2):
                chunk_part(j, a_hi, a_lo, KD, 1, range(KD)).then_inc(s_mm, 1)
            up(0, 2, R_S)
            up(0, 3, R_S + 1)
            with pe.Fori(1, NPAIR - 1) as i:
                up(i, 0, 6 * i + (R_S - 3))
                down(i - 1, 6 * i + (R_S - 1), f_hi, f_lo, wd_hi, wd_lo)
                up(i, 1, 6 * i + (R_S - 1))
                up(i, 2, 6 * i + R_S)
                up(i, 3, 6 * i + (R_S + 1))
            i = NPAIR - 1
            up(i, 0, 6 * i + (R_S - 3))
            up(i, 1, 6 * i + (R_S - 1))
            up(i, 2, 6 * i + R_S)
            up(i, 3, 6 * i + (R_S + 1))
            down(i - 1, 6 * i + (R_S - 1), f_hi, f_lo, wd_hi, wd_lo)
            down(i, 6 * i + (R_S + 4), fl_hi, fl_lo, wdl_hi, wdl_lo)


def kernel(x, g_mix, w_in, g_sgu, w_s, b_s, sinks, rel_bias, w_pa, w_pb, w_out, g_ffn, w_up, w_conv, b_conv,
           w_down, g_final):
    import numpy as np
    import concourse.bacc as bacc
    from concourse import bass_utils

    def stationary(w):
        k, n = w.shape
        return w.reshape(k // P, P, n // P, P).transpose(2, 1, 0, 3).reshape(n // P, P, k)

    def head_pairs(a):
        return np.ascontiguousarray(a.reshape(NKV, G, HD, -1).transpose(1, 0, 2, 3)).reshape(NH * HD, -1)

    wi = w_in[0]
    pu, pv, q, k, v, gates = np.split(wi, [AW, 2 * AW, 3 * AW, 3 * AW + P, 3 * AW + 2 * P], axis=1)
    q = head_pairs(q.T).T
    w_in_t = stationary(np.concatenate([pv, pu, v, k, q, gates], axis=1))

    dist = 2 * P - 1 - np.arange(RC + 1)
    valid = (dist >= 0) & (dist < WINDOW)
    exact = NBUCKET // 2
    d = np.clip(dist, 0, None)
    large = exact + (np.log(np.maximum(d, 1) / exact) / np.log(WINDOW / exact) * (NBUCKET - exact)).astype(np.int32)
    bucket = np.where(d < exact, d, np.minimum(large, NBUCKET - 1))
    rows = np.zeros((NBUCKET + 1, RC + 1), np.float32)
    rows[bucket[valid], np.nonzero(valid)[0]] = 1.0
    rows[NBUCKET, ~valid] = NEG

    arrays = {
        "x": x[0].reshape(NB, P, D), "g_mix": g_mix[0], "w_in": w_in_t, "g_sgu": g_sgu[0],
        "w_s": w_s[0].transpose(2, 0, 1), "b_s": b_s[0].reshape(-1), "sinks": sinks[0], "rel_bias": rel_bias,
        "bucket_rows": rows, "w_pa": stationary(w_pa[0]), "w_pb": stationary(head_pairs(w_pb[0])),
        "w_out": w_out[0].reshape(KD, P, D), "g_ffn": g_ffn[0], "w_up": stationary(w_up[0]),
        "conv": np.concatenate([w_conv[0], b_conv], axis=0).reshape(4, 2 * NF, P).transpose(2, 1, 0),
        "w_down": w_down[0].reshape(NF, P, D), "g_final": g_final,
    }
    arrays = {f"in_{n}": np.ascontiguousarray(a) for n, a in arrays.items()}
    nc = bacc.Bacc("TRN2", target_bir_lowering=False, num_devices=1)
    aps = [nc.dram_tensor(n, a.shape, mybir.dt.from_np(a.dtype), kind="ExternalInput").ap()
           for n, a in arrays.items()]
    o = nc.dram_tensor("out_0_dram", (NB, P, D), F32, kind="ExternalOutput").ap()
    hybrid_block(nc, *aps, o)
    r = bass_utils.run_bass_kernel_spmd(nc, [arrays], core_ids=[0])
    return r.results[0]["out_0_dram"].reshape(1, SEQ, D)
```
